# Optimizing a Trainium2 kernel written in Bass

```python
import math
import jax, jax.numpy as jnp
from jax import lax
import numpy as np

D_MODEL = 1024
BATCH = 1
SEQ = 1024
DEPTH = 1

ATTN_HEADS = 4
HEAD_DIM = 64
ATTN_WIDTH = ATTN_HEADS * 2 * HEAD_DIM
CONV_WIDTH = D_MODEL - ATTN_WIDTH
CONV_GROUPS = 8
CONV_K = 3
D_FF = 2816
ROPE_THETA = 10000.0
Q_BLOCK = 128
NORM_EPS = 1e-6
SUBLN_EPS = 1e-5
N_MOD = 9
IN_COLS = 3 * ATTN_WIDTH + 3 * CONV_WIDTH

kernel_name = "hymba_diffattn_shortconv_macaron_adaln"

def rmsnorm(x, g, eps=NORM_EPS):
    x32 = x.astype(jnp.float32)
    y = x32 * lax.rsqrt(jnp.mean(x32 * x32, axis=-1, keepdims=True) + eps)
    return (y * g.astype(jnp.float32)).astype(x.dtype)

def modulate(h, shift, scale):
    return h * (1.0 + scale[:, None, :]) + shift[:, None, :]

def swiglu(h, w1, w3, w2):
    return (jax.nn.silu(h @ w1) * (h @ w3)) @ w2

def rope_tables(seq, dim, dtype):
    inv = 1.0 / (ROPE_THETA ** (jnp.arange(0, dim, 2, dtype=jnp.float32) / dim))
    ang = jnp.arange(seq, dtype=jnp.float32)[:, None] * inv[None, :]
    ang = jnp.concatenate([ang, ang], axis=-1)
    return jnp.cos(ang).astype(dtype), jnp.sin(ang).astype(dtype)

def apply_rope(t, cos, sin):
    half = t.shape[-1] // 2
    t1, t2 = t[..., :half], t[..., half:]
    rot = jnp.concatenate([-t2, t1], axis=-1)
    return t * cos[None, :, None, None, :] + rot * sin[None, :, None, None, :]

def diff_attention(q, k, v, lam):
    b, s, h, _, dh = q.shape
    nb = s // Q_BLOCK
    scale = 1.0 / math.sqrt(dh)
    qb = q.reshape(b, nb, Q_BLOCK, h, 2, dh).transpose(1, 0, 2, 3, 4, 5)
    kpos = jnp.arange(s)
    lam32 = lam.astype(jnp.float32)

    def block(args):
        qblk, i = args
        sc = jnp.einsum('bqhcd,bkhcd->bhcqk', qblk, k,
                        preferred_element_type=jnp.float32) * scale
        qpos = i * Q_BLOCK + jnp.arange(Q_BLOCK)
        mask = kpos[None, :] <= qpos[:, None]
        sc = jnp.where(mask[None, None, None], sc, -jnp.inf)
        p = jax.nn.softmax(sc, axis=-1)
        p = p[:, :, 0] - lam32 * p[:, :, 1]
        return jnp.einsum('bhqk,bkhe->bqhe', p.astype(v.dtype), v)

    out = lax.map(block, (qb, jnp.arange(nb)))
    return out.transpose(1, 0, 2, 3, 4).reshape(b, s, h, v.shape[-1])

def causal_short_conv(u, w):
    ch = u.shape[-1]
    return lax.conv_general_dilated(
        u, w[:, None, :].astype(u.dtype), window_strides=(1,),
        padding=[(CONV_K - 1, 0)], dimension_numbers=('NWC', 'WIO', 'NWC'),
        feature_group_count=ch)

def hybrid_mixer(h, w_in, lq1, lk1, lq2, lk2, subln_g, conv_w, conv_norm_g, w_out,
                 cos, sin, lambda_init):
    b, s, _ = h.shape
    z = h @ w_in
    cuts = [ATTN_WIDTH, 2 * ATTN_WIDTH, 3 * ATTN_WIDTH,
            3 * ATTN_WIDTH + CONV_WIDTH, 3 * ATTN_WIDTH + 2 * CONV_WIDTH]
    q, k, v, gate_b, gate_c, u = jnp.split(z, cuts, axis=-1)
    q = apply_rope(q.reshape(b, s, ATTN_HEADS, 2, HEAD_DIM), cos, sin)
    k = apply_rope(k.reshape(b, s, ATTN_HEADS, 2, HEAD_DIM), cos, sin)
    v = v.reshape(b, s, ATTN_HEADS, 2 * HEAD_DIM)
    f32 = jnp.float32
    lam = (jnp.exp(jnp.sum(lq1.astype(f32) * lk1.astype(f32)))
           - jnp.exp(jnp.sum(lq2.astype(f32) * lk2.astype(f32))) + lambda_init)
    o = diff_attention(q, k, v, lam)
    o = rmsnorm(o, subln_g, SUBLN_EPS) * (1.0 - lambda_init)
    attn_out = o.reshape(b, s, ATTN_WIDTH)
    y = gate_b * causal_short_conv(gate_c * u, conv_w)
    gsz = CONV_WIDTH // CONV_GROUPS
    y = rmsnorm(y.reshape(b, s, CONV_GROUPS, gsz),
                conv_norm_g.reshape(CONV_GROUPS, gsz)).reshape(b, s, CONV_WIDTH)
    return jnp.concatenate([attn_out, y], axis=-1) @ w_out

def setup_inputs(seed: int = 0) -> dict:
    key = jax.random.key(seed)
    ks = iter(jax.random.split(key, 32))
    nrm = lambda shape, s: jax.random.normal(next(ks), shape, jnp.float32) * s
    gain = lambda shape: 1.0 + nrm(shape, 0.02)
    D = D_MODEL
    return {
        "x": nrm((BATCH, SEQ, D), 1.0),
        "c": nrm((BATCH, D), 1.0),
        "w_ada": nrm((DEPTH, D, N_MOD * D), D ** -0.5),
        "b_ada": nrm((DEPTH, N_MOD * D), 0.02),
        "w_ada_final": nrm((D, 2 * D), D ** -0.5),
        "b_ada_final": nrm((2 * D,), 0.02),
        "g_ffn1": gain((DEPTH, D)),
        "g_mix": gain((DEPTH, D)),
        "g_ffn2": gain((DEPTH, D)),
        "g_final": gain((D,)),
        "ffn1_w1": nrm((DEPTH, D, D_FF), D ** -0.5),
        "ffn1_w3": nrm((DEPTH, D, D_FF), D ** -0.5),
        "ffn1_w2": nrm((DEPTH, D_FF, D), D_FF ** -0.5),
        "ffn2_w1": nrm((DEPTH, D, D_FF), D ** -0.5),
        "ffn2_w3": nrm((DEPTH, D, D_FF), D ** -0.5),
        "ffn2_w2": nrm((DEPTH, D_FF, D), D_FF ** -0.5),
        "w_in": nrm((DEPTH, D, IN_COLS), D ** -0.5),
        "lambda_q1": nrm((DEPTH, HEAD_DIM), 0.1),
        "lambda_k1": nrm((DEPTH, HEAD_DIM), 0.1),
        "lambda_q2": nrm((DEPTH, HEAD_DIM), 0.1),
        "lambda_k2": nrm((DEPTH, HEAD_DIM), 0.1),
        "subln_g": gain((DEPTH, 2 * HEAD_DIM)),
        "conv_w": nrm((DEPTH, CONV_K, CONV_WIDTH), CONV_K ** -0.5),
        "conv_norm_g": gain((DEPTH, CONV_WIDTH)),
        "w_out": nrm((DEPTH, D, D), D ** -0.5),
    }

def reference(x, c, w_ada, b_ada, w_ada_final, b_ada_final, g_ffn1, g_mix, g_ffn2, g_final,
              ffn1_w1, ffn1_w3, ffn1_w2, ffn2_w1, ffn2_w3, ffn2_w2, w_in,
              lambda_q1, lambda_k1, lambda_q2, lambda_k2, subln_g, conv_w, conv_norm_g, w_out):
    s = x.shape[1]
    cos, sin = rope_tables(s, HEAD_DIM, x.dtype)
    c_act = jax.nn.silu(c)
    for l in range(DEPTH):
        lambda_init = 0.8 - 0.6 * math.exp(-0.3 * l)
        mod = c_act @ w_ada[l] + b_ada[l]
        sh1, sc1, gt1, sh2, sc2, gt2, sh3, sc3, gt3 = jnp.split(mod, N_MOD, axis=-1)
        h = modulate(rmsnorm(x, g_ffn1[l]), sh1, sc1)
        x = x + 0.5 * gt1[:, None, :] * swiglu(h, ffn1_w1[l], ffn1_w3[l], ffn1_w2[l])
        h = modulate(rmsnorm(x, g_mix[l]), sh2, sc2)
        x = x + gt2[:, None, :] * hybrid_mixer(
            h, w_in[l], lambda_q1[l], lambda_k1[l], lambda_q2[l], lambda_k2[l],
            subln_g[l], conv_w[l], conv_norm_g[l], w_out[l], cos, sin, lambda_init)
        h = modulate(rmsnorm(x, g_ffn2[l]), sh3, sc3)
        x = x + 0.5 * gt3[:, None, :] * swiglu(h, ffn2_w1[l], ffn2_w3[l], ffn2_w2[l])
    modf = c_act @ w_ada_final + b_ada_final
    shf, scf = jnp.split(modf, 2, axis=-1)
    return modulate(rmsnorm(x, g_final), shf, scf)


_drawn_inputs = setup_inputs


def setup_inputs(seed=0):
    import zlib

    import numpy as np

    out = dict(_drawn_inputs(seed))
    spreads = {}
    factors = {'g_ffn1': 7.423,
     'g_mix': 4.967,
     'g_ffn2': 24.688,
     'g_final': 30.426,
     'lambda_q1': 7.791,
     'lambda_k1': 200.0,
     'lambda_q2': 8.0,
     'lambda_k2': 8.0,
     'subln_g': 200.0,
     'conv_norm_g': 179.473,
     'b_ada_final': 3.233}
    for name, (base, spread) in spreads.items():
        noise = np.random.default_rng([zlib.crc32(name.encode()), seed]).standard_normal(out[name].shape)
        drawn = base * np.exp(spread * noise) if base else spread * noise
        out[name] = __import__('jax').numpy.asarray(drawn.astype(out[name].dtype))
    for name, factor in factors.items():
        out[name] = (out[name] * factor).astype(out[name].dtype)
    return out
```

```python
from contextlib import ExitStack

import concourse.bass as bass
from concourse import mybir

F32 = mybir.dt.float32
F32R = mybir.dt.float32r
ALU = mybir.AluOpType
ACT = mybir.ActivationFunctionType
AX = mybir.AxisListType

P = 128
D = 1024
S = 1024
KT = D // P
HALF = 512
NH = S // HALF
F = 2816
FT = F // P
GF = 2
NG = FT // GF
HEADS = 4
DH = 64
QB = S // P
EPS = 1e-6
SUB_EPS = 1e-5
LAMBDA_INIT = 0.8 - 0.6
MASKED = -3.0e38

RING = 3
ADA_RING = 4
BANKS = 6
SECTIONS = 11
SH1, SC1, GT1, SH2, SC2, GT2, SH3, SC3, GT3, SHF, SCF = range(SECTIONS)

U_FFN = NG * 3 * GF
U_CONV = U_FFN
U_V = U_CONV + 16
U_ATT = U_V + 4
U_FFN2 = U_ATT + 12
UNITS = U_FFN2 + U_FFN

JOBS = {"ffn1": 0}
EVAC = {"ffn1": 0}
AEVAC = {"ffn1": 0}
GDONE = {"ffn1": 0}
for _now, _next, _n, _j, _e, _a, _g in (("ffn1", "conv", NG, 24, 20, 4, 4), ("conv", "v", 2, 28, 24, 4, 4),
                                        ("v", "att", 1, 8, 4, 4, 0), ("att", "ffn2", HEADS, 20, 16, 0, 2),
                                        ("ffn2", "end", NG, 24, 20, 4, 4)):
    JOBS[_next] = JOBS[_now] + _n * _j
    EVAC[_next] = EVAC[_now] + _n * _e
    AEVAC[_next] = AEVAC[_now] + _n * _a
    GDONE[_next] = GDONE[_now] + _n * _g

COLS = {}
_at = 0
for _name, _n in (("b_ada", SECTIONS * KT), ("c", KT), ("g1", KT), ("g2", KT), ("g3", KT), ("gf", KT),
                  ("subln", 1), ("conv_w", 12), ("conv_g", 4)):
    COLS[_name] = (_at, _n)
    _at += _n
NCOLS = _at


def program(nc, units, ada, x_t, cols_d, lam_d, rope_d, square_d, out_t):
    ctx = ExitStack()
    with ctx:
        at = [16512]

        def place(name, shape, dtype=F32, like=None):
            size = 4
            for n in shape[1:]:
                size *= n
            offset = at[0] if like is None else like
            if like is None:
                at[0] += (size + 31) // 32 * 32
            return nc.alloc_sbuf_tensor_at(name, shape, dtype, offset=offset), offset

        X, _ = place("X", [P, KT, S])
        Hh, h_at = place("Hh", [P, KT, S], F32R)
        Hl, hl_at = place("Hl", [P, KT, S], F32R)
        Wr, _ = place("Wr", [P, RING, S])
        Wh, _ = place("Wh", [P, RING, S], F32R)
        Wl, _ = place("Wl", [P, RING, S], F32R)
        Gh, _ = place("Gh", [P, GF, S], F32R)
        Gl, _ = place("Gl", [P, GF, S], F32R)
        V, v_at = place("V", [P, QB, HEADS * P])
        Ada, _ = place("Ada", [P, ADA_RING, D], like=v_at)
        QK, qk_at = place("QK", [P, 2, S + 8])
        AdaSum, _ = place("AdaSum", [P, D], like=qk_at)
        CU, _ = place("CU", [P, S + 2], like=qk_at)
        CT, _ = place("CT", [P, S], like=qk_at + 4 * (S + 8))
        PR, pr_at = place("PR", [P, 3, S])
        SqSum, _ = place("SqSum", [P, NH, HALF], like=pr_at)
        Sq, _ = place("Sq", [P, 2, HALF], like=pr_at + 4 * S)
        Spread, _ = place("Spread", [P, NH, HALF], like=pr_at + 8 * S)
        Rope, _ = place("Rope", [P, 2, S])
        TmpA, tmp_at = place("TmpA", [P, 2, HALF])
        TmpG, _ = place("TmpG", [P, 2, HALF])
        DT, _ = place("DT", [P, 2, S], like=tmp_at)
        Lam4, _ = place("Lam4", [P, 4, DH], like=tmp_at)
        O, o_at = place("O", [P, QB, P])
        LamP, _ = place("LamP", [P, 2, DH], like=o_at)
        Square, _ = place("Square", [P, 2, P])
        Cols, _ = place("Cols", [P, NCOLS])
        Mod, _ = place("Mod", [P, SECTIONS * KT])
        Scale, _ = place("Scale", [P, 4, KT])
        Gate, _ = place("Gate", [P, 3, KT])
        CAct, _ = place("CAct", [P, KT])
        Ones, _ = place("Ones", [P, 1])
        Mean, _ = place("Mean", [P, 1])
        MeanG, _ = place("MeanG", [P, 2])
        EpsC, _ = place("EpsC", [P, 2])
        Root, _ = place("Root", [P, 8])
        Inv, _ = place("Inv", [P, 8])
        LamS, _ = place("LamS", [P, 8])
        SubG, _ = place("SubG", [P, 1])
        NMax, _ = place("NMax", [P, 2])
        Sum, _ = place("Sum", [P, 2])
        RSum, _ = place("RSum", [P, 2])
        SqO, _ = place("SqO", [P, QB])
        Out, _ = place("Out", [P, KT, S], like=h_at)
        XN, _ = place("XN", [P, KT, S], like=hl_at)
        assert at[0] <= nc.sbuf_usable_end

        PS = nc.alloc_psum_tensor("PS", [P, 8, HALF], F32)
        ident, mask = Square[:, 0, :], Square[:, 1, :]

        def col(name, i=0, n=1):
            a = COLS[name][0] + i
            return Cols[:, a:a + n]

        def half(h):
            return slice(h * HALF, (h + 1) * HALF)

        def blk(b):
            return slice(b * P, (b + 1) * P)

        def flat(ap):
            return ap.rearrange("p a b -> p (a b)")

        def scores(c, first, last):
            return flat(PS[:, 2 * c:2 * c + 2, :])[:, first * P:last * P]

        sems = {}

        def sem(name):
            sems[name] = ctx.enter_context(nc.semaphore(name))
            return sems[name]

        raw_loaded = [sem(f"raw_loaded{i}") for i in range(RING)]
        ada_loaded = [sem(f"ada_loaded{i}") for i in range(ADA_RING)]
        x_loaded = [sem(f"x_loaded{k}") for k in range(KT)]
        cols_loaded, square_loaded = sem("cols_loaded"), sem("square_loaded")
        lam_loaded, rope_loaded, out_stored = sem("lam_loaded"), sem("rope_loaded"), sem("out_stored")
        hi_done = sem("hi_done")
        lo_done = sem("lo_done")
        v_used = sem("v_used")
        job_done = sem("job_done")
        evac = sem("evac")
        aevac = sem("aevac")
        ghi = sem("ghi")
        g_ready = sem("g_ready")
        mset = sem("mset")
        halo = sem("halo")
        consts = sem("consts")
        c_act = sem("c_act")
        ada_used = sem("ada_used")
        cols_done = sem("cols_done")
        mod_done = sem("mod_done")
        scales = sem("scales")
        lam_done = sem("lam_done")
        lam_exp = sem("lam_exp")
        sq_done = sem("sq_done")
        ssum = sem("ssum")
        mean_done = sem("mean_done")
        root_done = sem("root_done")
        inv_done = sem("inv_done")
        spread_done = sem("spread_done")
        bcast_done = sem("bcast_done")
        xn_done = sem("xn_done")
        hh_done = sem("hh_done")
        h_ready = sem("h_ready")
        ct_done = sem("ct_done")
        csq_done, cmean_done, croot_done = sem("csq_done"), sem("cmean_done"), sem("croot_done")
        cinv_done, cspread_done, cbc_done = sem("cinv_done"), sem("cspread_done"), sem("cbc_done")
        cg_done = sem("cg_done")
        rraw = sem("rraw")
        rmul = sem("rmul")
        rope_done = sem("rope_done")
        score_done, masked, max_done = sem("score_done"), sem("masked"), sem("max_done")
        exp_done, rsum_done, scaled = sem("exp_done"), sem("rsum_done"), sem("scaled")
        diff_done = sem("diff_done")
        tr_done = sem("tr_done")
        dt_done = sem("dt_done")
        pv_done, o_done, osq_done = sem("pv_done"), sem("o_done"), sem("osq_done")
        oroot_done, oinv_done, onorm_done = sem("oroot_done"), sem("oinv_done"), sem("onorm_done")
        ot_done = sem("ot_done")
        ag_done = sem("ag_done")

        block = ctx.enter_context(nc.Block())

        @block.sync
        def _(sp):
            sp.wait_ge(ada_used, KT)
            for n in range(RING):
                sp.dma_start(Wr[:, n, :], units[n]).then_inc(raw_loaded[n], 16)
            sp.dma_start(Rope[:], rope_d).then_inc(rope_loaded, 16)
            with sp.Fori(1, UNITS // RING) as i:
                for s in range(RING):
                    sp.wait_ge(lo_done, i * RING + (s - RING + 1))
                    sp.dma_start(Wr[:, s, :], units[i * RING + s]).then_inc(raw_loaded[s], 16)
            for n in range(UNITS // RING * RING, UNITS):
                sp.wait_ge(lo_done, n - RING + 1)
                sp.dma_start(Wr[:, n % RING, :], units[n]).then_inc(raw_loaded[n % RING], 16)
            for h in range(NH):
                for k in range(KT):
                    sp.wait_ge(hh_done, (6 + h) * KT + k + 1)
                    sp.dma_start(out_t[k, :, half(h)], Out[:, k, half(h)]).then_inc(out_stored, 16)
            sp.wait_ge(out_stored, 16 * NH * KT)

        @block.gpsimd
        def _(pool):
            for r in range(ADA_RING):
                pool.dma_start(Ada[:, r, :], ada[r]).then_inc(ada_loaded[r], 16)
            with pool.Fori(1, SECTIONS * KT // ADA_RING) as i:
                for s in range(ADA_RING):
                    pool.wait_ge(ada_used, i * ADA_RING + (s - ADA_RING + 1))
                    pool.dma_start(Ada[:, s, :], ada[i * ADA_RING + s]).then_inc(ada_loaded[s], 16)

        @block.scalar
        def _(act):
            def split_hi(n, wait, value, i=0, per=0):
                act.wait_ge(wait, value)
                act.wait_ge(raw_loaded[n % RING], 16 * (n // RING + 1) + i * (16 * per // RING))
                nc.scalar.activation(Wh[:, n % RING, :], Wr[:, n % RING, :], ACT.Copy).then_inc(hi_done, 1)

            def g_hi(slot, h, wait, value):
                act.wait_ge(wait, value)
                nc.scalar.activation(Gh[:, slot, half(h)], TmpG[:, h, :], ACT.Copy).then_inc(ghi, 1)

            def square(q, d):
                if d >= 3:
                    act.wait_ge(ssum, q * (KT - 1) + d - 2)
                out = Sq[:, d % 2, :] if d else SqSum[:, q % NH, :]
                nc.scalar.activation(out, X[:, d, half(q % NH)], ACT.Square).then_inc(sq_done, 1)

            def root(q):
                act.wait_ge(mean_done, q + 1)
                nc.scalar.activation(Root[:, 4 * (q % 2):4 * (q % 2) + 4], PS[:, 6, 0:4], ACT.Sqrt, bias=EpsC[:, 0:1]).then_inc(root_done, 1)

            def norm_chunk(q, k, shift, out=None, xn=None):
                at = q * KT + k
                act.wait_ge(xn_done, at + 1)
                if out is None and at >= 2:
                    act.wait_ge(h_ready, at - 1)
                outs = (TmpG[:, k % 2, :], Hh[:, k, half(q % NH)]) if out is None else (out[:, k, half(q % NH)],)
                for o in outs:
                    made = nc.scalar.activation(o, TmpA[:, k % 2, :] if xn is None else xn, ACT.Identity,
                                                bias=Mod[:, shift * KT + k:shift * KT + k + 1],
                                                scale=Scale[:, q // NH, k:k + 1])
                made.then_inc(hh_done, 1)

            def norm_tiles(q0, shift, split=(), jobs=0, out=None):
                for k in range(KT):
                    norm_chunk(q0, k, shift, out)
                    if k == 1:
                        for n in split[:1]:
                            split_hi(n, job_done, jobs)
                        root(q0 + 1)
                for n in split[1:]:
                    split_hi(n, job_done, jobs)
                for k in range(KT):
                    norm_chunk(q0 + 1, k, shift, out)

            def tail_squares(q0, e_end):
                for h in range(NH):
                    for d in range(KT):
                        act.wait_ge(evac, e_end - (NH - h) * KT + d + 1)
                        square(q0 + h, d)
                        if h and d == 3:
                            root(q0)

            def ffn_group(phase, g, n0, first=False, final=False):
                J, E = JOBS[phase] + g * 24, EVAC[phase] + g * 20
                if first:
                    act.wait_ge(hh_done, (NH if phase == "ffn1" else 3 * NH) * KT)
                else:
                    for c in (1, 2):
                        split_hi(n0 + c, job_done, J, g, 6)
                for f in range(GF):
                    for h in range(NH):
                        q = f * NH + h
                        act.wait_ge(job_done, J + 2 * q + 1)
                        if q >= 2:
                            act.wait_ge(evac, E + q - 1)
                        nc.scalar.activation(TmpA[:, h, :], PS[:, (2 * q) % BANKS, :], ACT.Silu).then_inc(aevac, 1)
                        if h == 1:
                            split_hi(n0 + 3 + 2 * f, job_done, J + 2 * q + 1, g, 6)
                        g_hi(f, h, evac, E + q + 1)
                    if not (final and f == GF - 1):
                        split_hi(n0 + 4 + 2 * f, job_done, J + 4 * f + 4, g, 6)

            act.dma_start(Cols[:], cols_d).then_inc(cols_loaded, 16)
            act.dma_start(Lam4[:], lam_d).then_inc(lam_loaded, 16)
            for k in range(KT):
                act.dma_start(X[:, k, :], x_t[k]).then_inc(x_loaded[k], 16)
                if k == 1:
                    act.dma_start(Square[:], square_d).then_inc(square_loaded, 16)
            act.wait_ge(cols_loaded, 16)
            nc.scalar.activation(CAct[:], col("c", 0, KT), ACT.Silu).then_inc(c_act, 1)
            act.wait_ge(lam_done, 2)
            nc.scalar.activation(LamS[:, 2:4], LamS[:, 0:2], ACT.Exp).then_inc(lam_exp, 1)
            act.wait_ge(consts, 1)
            for d in range(KT):
                act.wait_ge(x_loaded[d], 16)
                for h in range(NH):
                    if d >= 2:
                        act.wait_ge(ssum, NH * (d - 2) + h + 1)
                    out = Sq[:, h, :] if d else SqSum[:, h, :]
                    nc.scalar.activation(out, X[:, d, half(h)], ACT.Square).then_inc(sq_done, 1)
            for q in range(NH):
                root(q)
            for n in range(RING):
                act.wait_ge(raw_loaded[n], 16)
                nc.scalar.activation(Wh[:, n, :], Wr[:, n, :], ACT.Copy).then_inc(hi_done, 1)
            act.wait_ge(scales, 1)
            act.wait_ge(xn_done, NH * KT)
            for q in range(NH):
                for k in range(KT):
                    norm_chunk(q, k, SH1, xn=XN[:, k, half(q)])

            ffn_group("ffn1", 0, 0, first=True)
            with act.Fori(1, NG) as g:
                ffn_group("ffn1", g, 0)
            act.wait_ge(scales, 7)
            tail_squares(2, EVAC["conv"])
            norm_tiles(2, SH2, (U_CONV + 1, U_CONV + 2), JOBS["conv"])

            for cg in range(2):
                J, E, n0 = JOBS["conv"] + 28 * cg, EVAC["conv"] + 24 * cg, U_CONV + 8 * cg

                def copy_u(q):
                    act.wait_ge(job_done, J + 3 * q + 1)
                    if q >= 2:
                        act.wait_ge(evac, E + 2 * q - 3)
                    nc.scalar.activation(TmpA[:, q % 2, :], PS[:, (3 * q) % BANKS, :], ACT.Copy).then_inc(aevac, 1)

                if cg:
                    for c in (1, 2):
                        split_hi(n0 + c, job_done, J)
                else:
                    act.wait_ge(hh_done, 2 * NH * KT)
                copy_u(0)
                for q in range(4):
                    jt, h, cq = q // 2, q % 2, 4 * cg + q
                    if h == 1:
                        split_hi(n0 + 3 * jt + 3, job_done, J + 3 * q + 1)
                        split_hi(n0 + 3 * jt + 4, job_done, J + 3 * q + 2)
                    act.wait_ge(evac, E + 2 * q + 2)
                    nc.scalar.activation(Sq[:, h, :], CT[:, half(h)], ACT.Square).then_inc(csq_done, 1)
                    if h == 1:
                        split_hi(n0 + 3 * jt + 5, job_done, J + 3 * q + 3)
                    act.wait_ge(cmean_done, cq + 1)
                    nc.scalar.activation(Root[:, 0:8], PS[:, 6, 0:8], ACT.Sqrt, bias=EpsC[:, 0:1])\
                        .then_inc(croot_done, 1)
                    if q < 3:
                        copy_u(q + 1)
                    g_hi(jt, h, cg_done, cq + 1)

            for c in (1, 2):
                split_hi(U_V + c, job_done, JOBS["v"])
            for c in (3, 4, 5):
                split_hi(U_V + c, v_used, c - 2)
            for t in range(0, QB, 2):
                act.wait_ge(job_done, JOBS["v"] + t + 1)
                nc.scalar.activation(V[:, t, :], PS[:, t, :], ACT.Copy).then_inc(aevac, 1)

            def head(hh):
                J = JOBS["att"] + hh * 20
                split_hi(U_ATT + 2, job_done, J, hh, 3)
                for j in range(4):
                    act.wait_ge(job_done, J + j + 1)
                    if j >= 2:
                        act.wait_ge(rmul, hh * 4 + j - 1)
                    nc.scalar.activation(TmpA[:, j % 2, :], PS[:, j, :], ACT.Copy,
                                         scale=DH ** -0.5 if j < 2 else 1.0).then_inc(rraw, 1)
                    if j % 2:
                        split_hi(U_ATT + 3 + j // 2, job_done, J + j + 1, hh, 3)

                def exps(i):
                    for c in range(2):
                        act.wait_ge(max_done, hh * (2 * QB) + 2 * i + c + 1)
                        nc.scalar.activation(PR[:, c, 0:P * (i + 1)], scores(c, 0, i + 1), ACT.Exp,
                                             bias=NMax[:, c:c + 1], accum_out=Sum[:, c:c + 1]).then_inc(exp_done, 1)

                def squares_o(i):
                    act.wait_ge(o_done, hh * QB + i + 1)
                    if i:
                        act.wait_ge(osq_done, hh * QB + i)
                    nc.scalar.activation(PS[:, 7, 0:P], O[:, i, :], ACT.Square, accum_out=SqO[:, i:i + 1])\
                        .then_inc(osq_done, 1)

                exps(0)
                for i in range(QB):
                    if i < QB - 1:
                        exps(i + 1)
                    act.wait_ge(tr_done, hh * QB + i + 1)
                    nc.scalar.activation(DT[:, i % 2, 0:P * (i + 1)], flat(PS[:, 4:6, :])[:, 0:P * (i + 1)],
                                         ACT.Copy).then_inc(dt_done, 1)
                    if i:
                        squares_o(i - 1)
                squares_o(QB - 1)
                act.wait_ge(osq_done, hh * QB + QB)
                nc.scalar.activation(Root[:, 0:QB], SqO[:], ACT.Sqrt, bias=EpsC[:, 1:2], scale=1.0 / P)\
                    .then_inc(oroot_done, 1)
                for h in range(NH):
                    act.wait_ge(ot_done, hh * NH + h + 1)
                    nc.scalar.activation(TmpG[:, h, :], PS[:, 4 + h, :], ACT.Copy, scale=SubG[:, 0:1])\
                        .then_inc(ag_done, 1)
                    g_hi(0, h, ag_done, hh * NH + h + 1)

            with act.Fori(0, HEADS - 1) as hh:
                head(hh)
            head(HEADS - 1)
            tail_squares(4, EVAC["ffn2"])
            norm_tiles(4, SH3, (U_FFN2 + 2,), JOBS["ffn2"])

            ffn_group("ffn2", 0, U_FFN2, first=True)
            with act.Fori(1, NG - 1) as g:
                ffn_group("ffn2", g, U_FFN2)
            ffn_group("ffn2", NG - 1, U_FFN2, final=True)
            tail_squares(6, EVAC["end"])
            norm_tiles(6, SHF, out=Out)

        @block.vector
        def _(dve):
            def split_lo(n, i=0, per=0):
                dve.wait_ge(hi_done, n + 1 + i * per)
                nc.vector.tensor_tensor(Wl[:, n % RING, :], Wr[:, n % RING, :], Wh[:, n % RING, :].bitcast(F32),
                                        ALU.subtract).then_inc(lo_done, 1)

            def g_lo(slot, h, count):
                dve.wait_ge(ghi, count)
                nc.vector.tensor_tensor(Gl[:, slot, half(h)], TmpG[:, h, :], Gh[:, slot, half(h)].bitcast(F32),
                                        ALU.subtract).then_inc(g_ready, 1)

            def ada_tile(s, k):
                dve.wait_ge(ada_loaded[k % ADA_RING], 16 * (s * (KT // ADA_RING) + k // ADA_RING + 1))
                w = Ada[:, k % ADA_RING, :]
                if k == 0:
                    if not (isinstance(s, int) and s == 0):
                        dve.wait_ge(cols_done, s)
                    nc.vector.tensor_scalar(AdaSum[:], w, CAct[:, 0:1], None, ALU.mult).then_inc(ada_used, 1)
                else:
                    dve.wait_ge(ada_used, s * KT + k)
                    nc.vector.scalar_tensor_tensor(AdaSum[:], w, CAct[:, k:k + 1], AdaSum[:], ALU.mult, ALU.add)\
                        .then_inc(ada_used, 1)

            def ada_bias(s):
                dve.wait_ge(cols_done, s + 1)
                nc.vector.tensor_tensor(Mod[:, bass.ts(s, KT)], PS[:, 7, 0:KT], Cols[:, bass.ts(s, KT)], ALU.add)\
                    .then_inc(mod_done, 1)

            def scale(n, section, gain):
                dve.wait_ge(mod_done, section + 1)
                nc.vector.scalar_tensor_tensor(Scale[:, n, :], Mod[:, bass.ts(section, KT)], 1.0, col(gain, 0, KT),
                                               ALU.add, ALU.mult).then_inc(scales, 1)

            def gate(n, section, factor):
                dve.wait_ge(mod_done, section + 1)
                nc.vector.tensor_scalar(Gate[:, n, :], Mod[:, bass.ts(section, KT)], factor, None, ALU.mult)\
                    .then_inc(scales, 1)

            def add_squares(q, d):
                dve.wait_ge(sq_done, q * KT + d + 1)
                if d >= 2:
                    dve.wait_ge(ssum, q * (KT - 1) + d - 1)
                nc.vector.tensor_tensor(SqSum[:, q % NH, :], SqSum[:, q % NH, :], Sq[:, d % 2, :], ALU.add)\
                    .then_inc(ssum, 1)

            def spread(q):
                dve.wait_ge(root_done, q + 1)
                part = slice(4 * (q % 2), 4 * (q % 2) + 4)
                nc.vector.reciprocal(Inv[:, part], Root[:, part]).then_inc(inv_done, 1)
                dve.wait_ge(inv_done, q + 1)
                nc.vector.tensor_copy(Spread[:, q % NH, :].rearrange("p (b c) -> p b c", b=4),
                                      Inv[:, part].unsqueeze(2).to_broadcast([P, 4, P])).then_inc(spread_done, 1)

            def norm_mul(q, k):
                at = q * KT + k
                if k == 0:
                    dve.wait_ge(bcast_done, q + 1)
                if at >= 2:
                    dve.wait_ge(hh_done, at - 1)
                nc.vector.tensor_tensor(TmpA[:, k % 2, :], X[:, k, half(q % NH)], PS[:, 7 - q % 2, :], ALU.mult)\
                    .then_inc(xn_done, 1)

            def norm_lo(q, k):
                dve.wait_ge(hh_done, q * KT + k + 1)
                nc.vector.tensor_tensor(Hl[:, k, half(q % NH)], TmpG[:, k % 2, :],
                                        Hh[:, k, half(q % NH)].bitcast(F32), ALU.subtract).then_inc(h_ready, 1)

            def norm_tiles(q0, split=(), final=False):
                for q in (q0, q0 + 1):
                    for k in range(KT):
                        norm_mul(q, k)
                        if k and not final:
                            norm_lo(q, k - 1)
                        if q == q0 and k == 2:
                            for n in split[:1]:
                                split_lo(n)
                        if q == q0 and k == 3:
                            spread(q0 + 1)
                    if not final:
                        norm_lo(q, KT - 1)
                    if q == q0:
                        for n in split[1:]:
                            split_lo(n)

            def add_out(job, n, t):
                h, d = t // KT, t % KT
                dve.wait_ge(job_done, job + t + 1)
                nc.vector.scalar_tensor_tensor(X[:, d, half(h)], PS[:, (job_bank + t) % BANKS, :], Gate[:, n, d:d + 1],
                                               X[:, d, half(h)], ALU.mult, ALU.add).then_inc(evac, 1)

            def add_outs(job, n, q0=None):
                for t in range(NH * KT):
                    add_out(job, n, t)
                    if q0 is None:
                        continue
                    q, d = q0 + t // KT, t % KT
                    if d >= 2:
                        add_squares(q, d - 1)
                    if d == KT - 1:
                        add_squares(q, d)
                    if t == KT + 5:
                        spread(q0)

            def ffn_group(phase, g, n0, n, first=False, final=False, ada=False, q0=None):
                nonlocal job_bank
                J, G, A = JOBS[phase] + g * 24, GDONE[phase] + g * 4, AEVAC[phase] + g * 4
                if first:
                    dve.wait_ge(h_ready, (NH if phase == "ffn1" else 3 * NH) * KT)
                else:
                    for c in (1, 2):
                        split_lo(n0 + c, g, 6)
                for f in range(GF):
                    for h in range(NH):
                        q = f * NH + h
                        if ada:
                            ada_tile(g + 2, 2 * q)
                            ada_tile(g + 2, 2 * q + 1)
                        if h == 1:
                            split_lo(n0 + 3 + 2 * f, g, 6)
                        dve.wait_ge(job_done, J + 2 * q + 2)
                        dve.wait_ge(aevac, A + q + 1)
                        nc.vector.tensor_tensor(TmpG[:, h, :], TmpA[:, h, :], PS[:, (2 * q + 1) % BANKS, :], ALU.mult)\
                            .then_inc(evac, 1)
                        g_lo(f, h, G + q + 1)
                    if not (final and f == GF - 1):
                        split_lo(n0 + 4 + 2 * f, g, 6)
                if ada:
                    ada_bias(g + 2)
                if first and n == 0:
                    gate(0, GT1, 0.5)
                    dve.wait_ge(scales, 2)
                job_bank = 8
                add_outs(J + 8, n, q0)

            job_bank = 0
            nc.vector.memset(Ones[:], 1.0)
            nc.vector.memset(Mean[:], 1.0 / D)
            nc.vector.memset(MeanG[:], 0.0).then_inc(mset, 1)
            nc.vector.memset(EpsC[:, 1:2], SUB_EPS)
            dve.wait_ge(mset, 1)
            for gi in range(2):
                nc.vector.memset(MeanG[gi * DH:(gi + 1) * DH, gi:gi + 1], 1.0 / DH)
            nc.vector.memset(EpsC[:, 0:1], EPS).then_inc(consts, 1)
            dve.wait_ge(lam_loaded, 16)
            nc.vector.tensor_tensor(LamP[:], Lam4[:, 0:2, :], Lam4[:, 2:4, :], ALU.mult).then_inc(lam_done, 1)
            dve.wait_ge(lam_done, 1)
            nc.vector.tensor_reduce(LamS[:, 0:2], LamP[:], AX.X, ALU.add).then_inc(lam_done, 1)
            dve.wait_ge(c_act, 1)
            for k in range(KT):
                ada_tile(SH1, k)
                for h in range(NH if k else 0):
                    dve.wait_ge(sq_done, NH * k + h + 1)
                    if k > 1:
                        dve.wait_ge(ssum, NH * (k - 2) + h + 1)
                    nc.vector.tensor_tensor(SqSum[:, h, :], SqSum[:, h, :], Sq[:, h, :], ALU.add).then_inc(ssum, 1)
            dve.wait_ge(lam_exp, 1)
            nc.vector.tensor_tensor(LamS[:, 4:5], LamS[:, 3:4], LamS[:, 2:3], ALU.subtract).then_inc(lam_done, 1)
            dve.wait_ge(lam_done, 3)
            nc.vector.tensor_scalar(LamS[:, 5:6], LamS[:, 4:5], -LAMBDA_INIT, None, ALU.add).then_inc(lam_done, 1)
            nc.vector.tensor_scalar(SubG[:], col("subln"), 1.0 - LAMBDA_INIT, None, ALU.mult).then_inc(lam_done, 1)
            ada_bias(SH1)
            for q in range(NH):
                spread(q)
            for k in range(KT):
                ada_tile(SC1, k)
                if k == 0:
                    dve.wait_ge(bcast_done, NH)
                for h in range(NH):
                    nc.vector.tensor_tensor(XN[:, k, half(h)], X[:, k, half(h)], PS[:, 7 - h, :], ALU.mult)\
                        .then_inc(xn_done, 1)
            ada_bias(SC1)
            scale(0, SC1, "g1")
            for n in range(RING - 1):
                split_lo(n)
            for q in range(NH):
                for k in range(KT):
                    norm_lo(q, k)
                    if q == 0 and k == KT - 1:
                        split_lo(RING - 1)

            ffn_group("ffn1", 0, 0, 0, first=True, ada=True)
            with dve.Fori(1, SECTIONS - 2) as g:
                ffn_group("ffn1", g, 0, 0, ada=True)
            for n, section, gain in ((1, SC2, "g2"), (2, SC3, "g3"), (3, SCF, "gf")):
                scale(n, section, gain)
            gate(1, GT2, 1.0)
            gate(2, GT3, 0.5)
            dve.wait_ge(scales, 7)
            ffn_group("ffn1", NG - 2, 0, 0)
            ffn_group("ffn1", NG - 1, 0, 0, q0=2)
            norm_tiles(2, (U_CONV + 1, U_CONV + 2))

            nc.vector.memset(CU[:, 0:2], 0.0).then_inc(halo, 1)
            dve.wait_ge(halo, 1)
            for cg in range(2):
                J, E, A, G = JOBS["conv"] + 28 * cg, EVAC["conv"] + 24 * cg, AEVAC["conv"] + 4 * cg, GDONE["conv"] + 4 * cg
                n0 = U_CONV + 8 * cg
                if cg:
                    for c in (1, 2):
                        split_lo(n0 + c)
                for q in range(4):
                    jt, h, cq = q // 2, q % 2, 4 * cg + q
                    tile = 2 * cg + jt
                    dve.wait_ge(job_done, J + 3 * q + 2)
                    dve.wait_ge(aevac, A + q + 1)
                    nc.vector.tensor_tensor(CU[:, 2 + h * HALF:2 + (h + 1) * HALF], TmpA[:, h, :],
                                            PS[:, (3 * q + 1) % BANKS, :], ALU.mult).then_inc(evac, 1)
                    dve.wait_ge(evac, E + 2 * q + 1)
                    nc.vector.tensor_scalar(CT[:, half(h)], CU[:, 2 + h * HALF:2 + (h + 1) * HALF],
                                            col("conv_w", 2 * 4 + tile), None, ALU.mult).then_inc(ct_done, 1)
                    for tap in (1, 0):
                        dve.wait_ge(ct_done, cq * 3 + 2 - tap)
                        nc.vector.scalar_tensor_tensor(CT[:, half(h)], CU[:, tap + h * HALF:tap + (h + 1) * HALF],
                                                       col("conv_w", tap * 4 + tile), CT[:, half(h)],
                                                       ALU.mult, ALU.add).then_inc(ct_done, 1)
                    if h == 1:
                        split_lo(n0 + 3 * jt + 3)
                        split_lo(n0 + 3 * jt + 4)
                    dve.wait_ge(job_done, J + 3 * q + 3)
                    dve.wait_ge(ct_done, cq * 3 + 3)
                    nc.vector.tensor_tensor(CT[:, half(h)], CT[:, half(h)], PS[:, (3 * q + 2) % BANKS, :], ALU.mult)\
                        .then_inc(evac, 1)
                    if h == 1:
                        split_lo(n0 + 3 * jt + 5)
                    dve.wait_ge(croot_done, cq + 1)
                    nc.vector.reciprocal(Inv[:, 0:8], Root[:, 0:8]).then_inc(cinv_done, 1)
                    dve.wait_ge(cinv_done, cq + 1)
                    nc.vector.tensor_copy(Spread[:, h, :].rearrange("p (b c) -> p b c", b=8),
                                          Inv[:, 0:8].unsqueeze(2).to_broadcast([P, 8, DH])).then_inc(cspread_done, 1)
                    dve.wait_ge(cbc_done, cq + 1)
                    nc.vector.scalar_tensor_tensor(TmpG[:, h, :], CT[:, half(h)], col("conv_g", tile), PS[:, 7, :],
                                                   ALU.mult, ALU.mult).then_inc(cg_done, 1)
                    g_lo(jt, h, G + q + 1)
                job_bank = 12
                add_outs(J + 12, 1)

            for c in range(1, 6):
                split_lo(U_V + c)
            for t in range(1, QB, 2):
                dve.wait_ge(job_done, JOBS["v"] + t + 1)
                nc.vector.tensor_copy(V[:, t, :], PS[:, t, :]).then_inc(evac, 1)

            def head(hh, q0=None):
                nonlocal job_bank
                split_lo(U_ATT + 2, hh, 3)
                for j in range(4):
                    to = QK[:, j // 2, half(j % 2)]
                    dve.wait_ge(rraw, hh * 4 + j + 1)
                    nc.vector.tensor_tensor(to, TmpA[:, j % 2, :], Rope[:, 0, half(j % 2)], ALU.mult)
                    for a in range(0, P, 32):
                        b = a ^ 32
                        made = nc.vector.scalar_tensor_tensor(
                            TmpG[a:a + 32, j % 2, :], PS[b:b + 32, j, :], DH ** -0.5 if j < 2 else 1.0,
                            Rope[b:b + 32, 1, half(j % 2)], ALU.mult, ALU.mult)
                    made.then_inc(rmul, 1)
                    dve.wait_ge(rmul, hh * 4 + j + 1)
                    nc.vector.tensor_tensor(to, to, TmpG[:, j % 2, :], ALU.add).then_inc(rope_done, 1)
                    if j % 2:
                        split_lo(U_ATT + 3 + j // 2, hh, 3)

                def maxima(i):
                    for c in range(2):
                        at = hh * (2 * QB) + 2 * i + c + 1
                        dve.wait_ge(score_done, at)
                        nc.vector.tensor_tensor(scores(c, i, i + 1), scores(c, i, i + 1), mask, ALU.add)\
                            .then_inc(masked, 1)
                        dve.wait_ge(masked, at)
                        nc.vector.tensor_reduce(NMax[:, c:c + 1], scores(c, 0, i + 1), AX.X, ALU.max, negate=True)\
                            .then_inc(max_done, 1)

                def copy_o(i):
                    dve.wait_ge(pv_done, hh * QB + i + 1)
                    nc.vector.tensor_copy(O[:, i, :], PS[:, 6, 0:P]).then_inc(o_done, 1)

                maxima(0)
                for i in range(QB):
                    at, w = hh * QB + i, P * (i + 1)
                    dve.wait_ge(exp_done, 2 * at + 2)
                    nc.vector.reciprocal(RSum[:], Sum[:]).then_inc(rsum_done, 1)
                    dve.wait_ge(rsum_done, at + 1)
                    nc.vector.tensor_scalar(PR[:, 1, 0:w], PR[:, 1, 0:w], RSum[:, 1:2], LamS[:, 5:6], ALU.mult, ALU.mult)\
                        .then_inc(scaled, 1)
                    if i:
                        dve.wait_ge(tr_done, at)
                    dve.wait_ge(scaled, at + 1)
                    nc.vector.scalar_tensor_tensor(PR[:, 2, 0:w], PR[:, 0, 0:w], RSum[:, 0:1], PR[:, 1, 0:w],
                                                   ALU.mult, ALU.add).then_inc(diff_done, 1)
                    if i < QB - 1:
                        maxima(i + 1)
                    if i:
                        copy_o(i - 1)
                copy_o(QB - 1)
                dve.wait_ge(oroot_done, hh + 1)
                nc.vector.reciprocal(Inv[:, 0:QB], Root[:, 0:QB]).then_inc(oinv_done, 1)
                dve.wait_ge(oinv_done, hh + 1)
                nc.vector.tensor_tensor(O[:], O[:], Inv[:, 0:QB].unsqueeze(2).to_broadcast([P, QB, P]), ALU.mult)\
                    .then_inc(onorm_done, 1)
                for h in range(NH):
                    g_lo(0, h, GDONE["att"] + hh * NH + h + 1)
                job_bank = 0
                add_outs(JOBS["att"] + hh * 20 + 4, 1, q0)

            with dve.Fori(0, HEADS - 1) as hh:
                head(hh)
            head(HEADS - 1, q0=4)
            norm_tiles(4, (U_FFN2 + 2,))

            ffn_group("ffn2", 0, U_FFN2, 2, first=True)
            with dve.Fori(1, NG - 1) as g:
                ffn_group("ffn2", g, U_FFN2, 2)
            ffn_group("ffn2", NG - 1, U_FFN2, 2, final=True, q0=6)
            norm_tiles(6, final=True)

        @block.tensor
        def _(pe):
            def mm(out, lhs, rhs, first, last):
                return nc.tensor.matmul(out, lhs, rhs, start=first, stop=last)

            def products(bank, n, h, ks):
                for k in ks:
                    s, w = n % RING, blk(k)
                    mm(PS[:, bank, :], Wh[:, s, w], Hh[:, k, half(h)], k == 0, False)
                    mm(PS[:, bank, :], Wh[:, s, w], Hl[:, k, half(h)], False, False)
                    made = mm(PS[:, bank, :], Wl[:, s, w], Hh[:, k, half(h)], False, k == KT - 1)
                    if k == KT - 1:
                        made.then_inc(job_done, 1)

            def project(bank, n, h):
                products(bank, n, h, range(KT))

            LAG = 3

            def project_new(bank, n, h, q):
                for k in range(KT + LAG):
                    if k < KT:
                        pe.wait_ge(h_ready, q * KT + k + 1)
                        products(bank, n, h, (k,))
                    if k >= LAG:
                        if k == LAG:
                            pe.wait_ge(lo_done, n + 2)
                        products(bank + 1, n + 1, h, (k - LAG,))
                    if k == 4 and q % 2 == 0 and q:
                        bcast(q + 1)

            def out_job(bank, ns, t):
                h, d = t // KT, t % KT
                for f, n in enumerate(ns):
                    s, w = n % RING, blk(d)
                    mm(PS[:, bank, :], Wh[:, s, w], Gh[:, f, half(h)], f == 0, False)
                    mm(PS[:, bank, :], Wh[:, s, w], Gl[:, f, half(h)], False, False)
                    made = mm(PS[:, bank, :], Wl[:, s, w], Gh[:, f, half(h)], False, f == len(ns) - 1)
                made.then_inc(job_done, 1)

            def mean(q):
                pe.wait_ge(ssum, (q + 1) * (KT - 1) if q >= NH else NH * (KT - 1))
                for b in range(4):
                    made = mm(PS[:, 6, b:b + 1], SqSum[:, q % NH, blk(b)], Mean[:], True, True)
                made.then_inc(mean_done, 1)

            def bcast(q):
                pe.wait_ge(spread_done, q + 1)
                for b in range(4):
                    made = mm(PS[:, 7 - q % 2, blk(b)], Spread[:, q % NH, blk(b)], ident, True, True)
                made.then_inc(bcast_done, 1)

            def ada_cols(s):
                pe.wait_ge(ada_used, s * KT + KT)
                for c in range(KT):
                    made = mm(PS[:, 7, c:c + 1], AdaSum[:, blk(c)], Ones[:], True, True)
                made.then_inc(cols_done, 1)

            def norm_between(q0, t):
                if q0 is not None and t == KT + 2:
                    mean(q0)
                if q0 is not None and t == KT + 6:
                    bcast(q0)

            def ffn_group(phase, g, n0, first=False, ada=False, q=None, q0=None):
                J, E, A, G = JOBS[phase] + g * 24, EVAC[phase] + g * 20, AEVAC[phase] + g * 4, GDONE[phase] + g * 4

                def bank_free(L):
                    if L < BANKS:
                        if not first:
                            pe.wait_ge(evac, E - 5 + L)
                        elif EVAC[phase]:
                            pe.wait_ge(evac, E)
                    elif L < BANKS + 8:
                        pe.wait_ge(*((evac, E + (L - BANKS) // 2 + 1) if L % 2 else (aevac, A + (L - BANKS) // 2 + 1)))
                    else:
                        pe.wait_ge(evac, E + 4 + L - 14 + 1)

                for f in range(GF):
                    for h in range(NH):
                        for w in range(2):
                            L = 4 * f + 2 * h + w
                            bank_free(L)
                            if q is not None and f == 0:
                                if w == 0:
                                    pe.wait_ge(lo_done, n0 + 1)
                                    bank_free(L + 1)
                                    project_new(L, n0, h, q + h)
                                continue
                            if h == 0:
                                pe.wait_ge(lo_done, n0 + 2 * f + w + 1 + g * 6)
                            project(L % BANKS, n0 + 2 * f + w, h)
                if ada:
                    ada_cols(g + 2)
                pe.wait_ge(lo_done, n0 + 6 + g * 6)
                for t in range(NH * KT):
                    bank_free(8 + t)
                    if t % KT == 0:
                        pe.wait_ge(g_ready, G + 3 + t // KT)
                    out_job((8 + t) % BANKS, (n0 + 4, n0 + 5), t)
                    norm_between(q0, t)
                if q0 is not None:
                    mean(q0 + 1)

            pe.wait_ge(consts, 1)
            ada_cols(SH1)
            pe.wait_ge(square_loaded, 16)
            pe.wait_ge(mod_done, 1)
            mean(0)
            pe.wait_ge(root_done, 1)
            mean(1)
            bcast(0)
            bcast(1)
            pe.wait_ge(xn_done, NH * KT)
            ada_cols(SC1)
            ffn_group("ffn1", 0, 0, first=True, ada=True, q=0)
            with pe.Fori(1, SECTIONS - 2) as g:
                ffn_group("ffn1", g, 0, ada=True)
            ffn_group("ffn1", NG - 2, 0)
            ffn_group("ffn1", NG - 1, 0, q0=2)

            for cg in range(2):
                J, E, A, G = JOBS["conv"] + 28 * cg, EVAC["conv"] + 24 * cg, AEVAC["conv"] + 4 * cg, GDONE["conv"] + 4 * cg
                n0 = U_CONV + 8 * cg

                def reader(L):
                    q, w = L // 3, L % 3
                    if L >= 12:
                        return evac, E + 8 + L - 12 + 1
                    return (evac, E + 2 * q + w) if w else (aevac, A + q + 1)

                def group_mean(q):
                    pe.wait_ge(csq_done, 4 * cg + q + 1)
                    for b in range(4):
                        made = mm(PS[:, 6, 2 * b:2 * b + 2], Sq[:, q % 2, blk(b)], MeanG[:], True, True)
                    made.then_inc(cmean_done, 1)

                def group_bcast(q):
                    pe.wait_ge(cspread_done, 4 * cg + q + 1)
                    for b in range(4):
                        made = mm(PS[:, 7, blk(b)], Spread[:, q % 2, blk(b)], ident, True, True)
                    made.then_inc(cbc_done, 1)

                for L in range(12):
                    q, w = L // 3, L % 3
                    if L < BANKS:
                        pe.wait_ge(evac, E)
                    else:
                        pe.wait_ge(*reader(L - BANKS))
                    if cg == 0 and q < 2 and w < 2:
                        if w == 0:
                            pe.wait_ge(lo_done, n0 + 1)
                            project_new(L, n0, q, 2 + q)
                    else:
                        if q % 2 == 0:
                            pe.wait_ge(lo_done, n0 + 3 * (q // 2) + w + 1)
                        project(L % BANKS, n0 + 3 * (q // 2) + w, q % 2)
                    if q and w == 0:
                        group_mean(q - 1)
                    if q and w == 1:
                        group_bcast(q - 1)
                pe.wait_ge(lo_done, n0 + 8)
                for t in range(NH * KT):
                    pe.wait_ge(*reader(12 + t - BANKS))
                    if t % KT == 0:
                        pe.wait_ge(g_ready, G + 3 + t // KT)
                    out_job((12 + t) % BANKS, (n0 + 6, n0 + 7), t)
                    if t == 1:
                        group_mean(3)
                    if t == 4:
                        group_bcast(3)

            pe.wait_ge(evac, EVAC["v"])
            for u in range(4):
                pe.wait_ge(lo_done, U_V + u + 1)
                s = (U_V + u) % RING
                for kk in range(2):
                    k, w = 2 * u + kk, half(kk)
                    for t in range(QB):
                        mm(PS[:, t, :], Hh[:, k, blk(t)], Wh[:, s, w], k == 0, False)
                        mm(PS[:, t, :], Hl[:, k, blk(t)], Wh[:, s, w], False, False)
                        made = mm(PS[:, t, :], Hh[:, k, blk(t)], Wl[:, s, w], False, k == KT - 1)
                        if k == KT - 1:
                            made.then_inc(job_done, 1)
                if u < 3:
                    made.then_inc(v_used, 1)

            def head(hh, q0=None):
                E = EVAC["att"] + hh * 16
                pe.wait_ge(aevac, AEVAC["att"])
                pe.wait_ge(evac, E)
                for j in range(4):
                    if j % 2 == 0:
                        pe.wait_ge(lo_done, U_ATT + j // 2 + 1 + hh * 3)
                    project(j, U_ATT + j // 2, j % 2)

                def score(i):
                    for c in range(2):
                        if i:
                            pe.wait_ge(exp_done, hh * (2 * QB) + 2 * i - 1 + c)
                        part = slice(c * DH, (c + 1) * DH)
                        for a in range(0, P * (i + 1), HALF):
                            b = min(a + HALF, P * (i + 1))
                            made = mm(PS[:, 2 * c + a // HALF, 0:b - a], QK[part, 0, blk(i)], QK[part, 1, a:b], True, True)
                        made.then_inc(score_done, 1)

                def values(i):
                    pe.wait_ge(dt_done, hh * QB + i + 1)
                    if i:
                        pe.wait_ge(o_done, hh * QB + i)
                    for b in range(i + 1):
                        made = mm(PS[:, 6, 0:P], DT[:, i % 2, blk(b)], V[:, b, bass.ts(hh, P)], b == 0, b == i)
                    made.then_inc(pv_done, 1)

                pe.wait_ge(rope_done, hh * 4 + 4)
                score(0)
                for i in range(QB):
                    if i < QB - 1:
                        score(i + 1)
                    pe.wait_ge(diff_done, hh * QB + i + 1)
                    if i:
                        pe.wait_ge(dt_done, hh * QB + i)
                    for b in range(i + 1):
                        made = nc.tensor.transpose(PS[:, 4 + b // 4, blk(b % 4)], PR[:, 2, blk(b)], ident)
                    made.then_inc(tr_done, 1)
                    if i:
                        values(i - 1)
                values(QB - 1)
                pe.wait_ge(onorm_done, hh + 1)
                for i in range(QB):
                    made = nc.tensor.transpose(PS[:, 4 + i // 4, blk(i % 4)], O[:, i, :], ident)
                    if i % 4 == 3:
                        made.then_inc(ot_done, 1)
                pe.wait_ge(lo_done, U_ATT + 3 + hh * 3)
                for t in range(NH * KT):
                    if t % KT == 0:
                        pe.wait_ge(g_ready, GDONE["att"] + hh * NH + t // KT + 1)
                    if t == 4:
                        pe.wait_ge(ag_done, hh * NH + 2)
                    if t >= BANKS:
                        pe.wait_ge(evac, E + t - BANKS + 1)
                    out_job(t % BANKS, (U_ATT + 2,), t)
                    norm_between(q0, t)

            with pe.Fori(0, HEADS - 1) as hh:
                head(hh)
            head(HEADS - 1, q0=4)
            mean(5)

            ffn_group("ffn2", 0, U_FFN2, first=True, q=4)
            with pe.Fori(1, NG - 1) as g:
                ffn_group("ffn2", g, U_FFN2)
            ffn_group("ffn2", NG - 1, U_FFN2, q0=6)
            bcast(7)


def kernel(**inputs):
    import numpy as np
    import concourse.bacc as bacc
    from concourse.bass_utils import run_bass_kernel_spmd

    a = {k: np.asarray(v) for k, v in inputs.items()}

    def cols(w, at):
        return w[:, at:at + P].reshape(KT, P, P).transpose(1, 0, 2).reshape(P, D)

    def rows(w, n):
        return w[n * P:(n + 1) * P]

    w_in, w_out = a["w_in"][0], a["w_out"][0]
    width = HEADS * P
    V0, B0, C0, U0 = 2 * width, 3 * width, 4 * width, 5 * width
    units = []

    def ffn_units(w1, w3, w2):
        for g in range(NG):
            for f in range(GF * g, GF * g + GF):
                units.extend([cols(w1, f * P), cols(w3, f * P)])
            units.extend(rows(w2, f) for f in range(GF * g, GF * g + GF))

    ffn_units(a["ffn1_w1"][0], a["ffn1_w3"][0], a["ffn1_w2"][0])
    for cg in range(2):
        for t in (2 * cg, 2 * cg + 1):
            units.extend(cols(w_in, at + t * P) for at in (U0, C0, B0))
        units.extend(rows(w_out, HEADS + t) for t in (2 * cg, 2 * cg + 1))
    for u in range(4):
        units.append(w_in[2 * u * P:(2 * u + 2) * P, V0:V0 + width].reshape(2, P, width).transpose(1, 0, 2).reshape(P, D))
    for h in range(HEADS):
        units.extend([cols(w_in, h * P), cols(w_in, width + h * P), rows(w_out, h)])
    ffn_units(a["ffn2_w1"][0], a["ffn2_w3"][0], a["ffn2_w2"][0])

    ada_w = np.concatenate([a["w_ada"][0], a["w_ada_final"]], axis=1)
    ada_b = np.concatenate([a["b_ada"][0], a["b_ada_final"]])

    def down(v):
        return v.reshape(-1, P).T

    inv = (1.0 / (np.float32(10000.0) ** (np.arange(0, DH, 2, dtype=np.float32) / np.float32(DH)))).astype(np.float32)
    ang = (np.arange(S, dtype=np.float32)[:, None] * inv[None, :]).astype(np.float32)
    cos, sin = np.cos(ang).T, np.sin(ang).T
    rope = np.stack([np.concatenate([cos] * 4), np.concatenate([sin, -sin] * 2)], axis=1)
    below = np.where(np.arange(P)[None, :] <= np.arange(P)[:, None], 0.0, MASKED)
    arrays = {
        "units": np.stack(units),
        "ada": ada_w.reshape(KT, P, SECTIONS, D).transpose(2, 0, 1, 3).reshape(SECTIONS * KT, P, D),
        "x_t": a["x"][0].T.reshape(KT, P, S),
        "cols": np.concatenate([down(ada_b), down(a["c"][0]), down(a["g_ffn1"][0]), down(a["g_mix"][0]),
                                down(a["g_ffn2"][0]), down(a["g_final"]), down(a["subln_g"][0]),
                                down(a["conv_w"][0].reshape(-1)), down(a["conv_norm_g"][0])], axis=1),
        "lam": np.broadcast_to(np.stack([a["lambda_q1"][0], a["lambda_q2"][0], a["lambda_k1"][0],
                                         a["lambda_k2"][0]])[None], (P, 4, DH)),
        "rope": rope.astype(np.float32),
        "square": np.stack([np.eye(P), below], axis=1).astype(np.float32),
    }
    arrays = {k: np.ascontiguousarray(v) for k, v in arrays.items()}
    nc = bacc.Bacc("TRN2", target_bir_lowering=False, num_devices=1)
    aps = [nc.dram_tensor(k, v.shape, mybir.dt.from_np(v.dtype), kind="ExternalInput").ap() for k, v in arrays.items()]
    out_t = nc.dram_tensor("out_t", (KT, P, S), F32, kind="ExternalOutput").ap()
    program(nc, *aps, out_t)
    got = run_bass_kernel_spmd(nc, [arrays], core_ids=[0])
    return np.ascontiguousarray(got.results[0]["out_t"].reshape(D, S).T)[None]
```

```python
from contextlib import ExitStack

import concourse.bass as bass
from concourse import mybir

F32 = mybir.dt.float32
F32R = mybir.dt.float32r
ALU = mybir.AluOpType
ACT = mybir.ActivationFunctionType
AX = mybir.AxisListType

P = 128
D = 1024
S = 1024
KT = D // P
HALF = 512
NH = S // HALF
F = 2816
FT = F // P
GF = 2
NG = FT // GF
HEADS = 4
DH = 64
QB = S // P
EPS = 1e-6
SUB_EPS = 1e-5
LAMBDA_INIT = 0.8 - 0.6
MASKED = -3.0e38

RING = 3
ADA_RING = 4
BANKS = 6
SECTIONS = 11
SH1, SC1, GT1, SH2, SC2, GT2, SH3, SC3, GT3, SHF, SCF = range(SECTIONS)

U_FFN = NG * 3 * GF
U_CONV = U_FFN
U_Q0 = U_CONV + 16
U_V = U_Q0 + 2
U_Q1 = U_V + 4
U_HEAD = U_Q1 + 2
U_WO2 = U_HEAD + 6
U_FFN2 = U_WO2 + 2
UNITS = U_FFN2 + U_FFN

JOBS = {"ffn1": 0}
EVAC = {"ffn1": 0}
AEVAC = {"ffn1": 0}
GDONE = {"ffn1": 0}
for _now, _next, _n, _j, _e, _a, _g in (("ffn1", "conv", NG, 24, 20, 4, 4), ("conv", "v", 2, 28, 24, 4, 4),
                                        ("v", "att", 1, 12, 4, 4, 0), ("att", "ffn2", HEADS, 19, 16, 0, 2),
                                        ("ffn2", "end", NG, 24, 20, 4, 4)):
    JOBS[_next] = JOBS[_now] + _n * _j
    EVAC[_next] = EVAC[_now] + _n * _e
    AEVAC[_next] = AEVAC[_now] + _n * _a
    GDONE[_next] = GDONE[_now] + _n * _g

CHUNKS = (7, 7, 6, 6, 6, 0, 0, 0)
TILES = (0, 0, 0, 0, 0, 5, 5, 6)
TILES_LAST = (0, 0, 2, 2, 3, 3, 3, 3)
assert sum(CHUNKS) == 2 * NH * KT and sum(TILES) == sum(TILES_LAST) == NH * KT
STEP_OF_JOB = [next(i for i in range(QB) if sum(CHUNKS[:i + 1]) >= KT * (j + 1)) for j in range(4)]
ROUNDS = [b // 4 + 1 for b in range(QB)]
DT_COUNT = [sum(ROUNDS[:b + 1]) for b in range(QB)]
ALL_ROUNDS = DT_COUNT[-1]

COLS = {}
_at = 0
for _name, _n in (("b_ada", SECTIONS * KT), ("c", KT), ("g1", KT), ("g2", KT), ("g3", KT), ("gf", KT),
                  ("subln", 1), ("conv_w", 12), ("conv_g", 4)):
    COLS[_name] = (_at, _n)
    _at += _n
NCOLS = _at


def program(nc, units, ada, x_t, cols_d, lam_d, rope_d, square_d, out_t):
    ctx = ExitStack()
    with ctx:
        at = [16512]

        def place(name, shape, dtype=F32, like=None):
            size = 4
            for n in shape[1:]:
                size *= n
            offset = at[0] if like is None else like
            if like is None:
                at[0] += (size + 31) // 32 * 32
            return nc.alloc_sbuf_tensor_at(name, shape, dtype, offset=offset), offset

        X, _ = place("X", [P, KT, S])
        Hh, h_at = place("Hh", [P, KT, S], F32R)
        Hl, hl_at = place("Hl", [P, KT, S], F32R)
        Wr, _ = place("Wr", [P, RING, S])
        Wh, _ = place("Wh", [P, RING, S], F32R)
        Wl, _ = place("Wl", [P, RING, S], F32R)
        Gh, gh_at = place("Gh", [P, GF, S], F32R)
        Gl, gl_at = place("Gl", [P, GF, S], F32R)
        NextQ, _ = place("NextQ", [P, S], like=gh_at + 4 * S)
        NextK, _ = place("NextK", [P, S], like=gl_at + 4 * S)
        V, v_at = place("V", [P, QB, HEADS * P])
        Ada, _ = place("Ada", [P, ADA_RING, D], like=v_at)
        QK, qk_at = place("QK", [P, 2, S + 8])
        AdaSum, _ = place("AdaSum", [P, D], like=qk_at)
        CU, _ = place("CU", [P, S + 2], like=qk_at)
        CT, _ = place("CT", [P, S], like=qk_at + 4 * (S + 8))
        PR, pr_at = place("PR", [P, 3, S])
        SqSum, _ = place("SqSum", [P, NH, HALF], like=pr_at)
        Sq, _ = place("Sq", [P, 2, HALF], like=pr_at + 4 * S)
        Spread, _ = place("Spread", [P, NH, HALF], like=pr_at + 8 * S)
        Rope, _ = place("Rope", [P, 2, S])
        TmpA, tmp_at = place("TmpA", [P, 2, HALF])
        TmpG, _ = place("TmpG", [P, 2, HALF])
        DT, _ = place("DT", [P, S], like=tmp_at + 4 * S)
        Lam4, _ = place("Lam4", [P, 4, DH], like=tmp_at)
        O, o_at = place("O", [P, QB, P])
        LamP, _ = place("LamP", [P, 2, DH], like=o_at)
        Square, _ = place("Square", [P, 2, P])
        Cols, _ = place("Cols", [P, NCOLS])
        Mod, _ = place("Mod", [P, SECTIONS * KT])
        Scale, _ = place("Scale", [P, 4, KT])
        Gate, _ = place("Gate", [P, 3, KT])
        CAct, _ = place("CAct", [P, KT])
        Ones, _ = place("Ones", [P, 1])
        Mean, _ = place("Mean", [P, 1])
        MeanG, _ = place("MeanG", [P, 2])
        EpsC, _ = place("EpsC", [P, 2])
        Root, _ = place("Root", [P, 8])
        Inv, _ = place("Inv", [P, 8])
        LamS, _ = place("LamS", [P, 8])
        SubG, _ = place("SubG", [P, 1])
        NMax, _ = place("NMax", [P, 2])
        Sum, _ = place("Sum", [P, 2])
        RSum, _ = place("RSum", [P, QB, 2])
        Ratio, _ = place("Ratio", [P, 1])
        Junk, _ = place("Junk", [P, P])
        SqO, _ = place("SqO", [P, QB])
        Out, _ = place("Out", [P, KT, S], like=h_at)
        XN, _ = place("XN", [P, KT, S], like=hl_at)
        assert at[0] <= nc.sbuf_usable_end

        PS = nc.alloc_psum_tensor("PS", [P, 8, HALF], F32)
        ident, mask = Square[:, 0, :], Square[:, 1, :]

        def col(name, i=0, n=1):
            a = COLS[name][0] + i
            return Cols[:, a:a + n]

        def half(h):
            return slice(h * HALF, (h + 1) * HALF)

        def blk(b):
            return slice(b * P, (b + 1) * P)

        def flat(ap):
            return ap.rearrange("p a b -> p (a b)")

        def scores(c, first, last):
            return flat(PS[:, 2 * c:2 * c + 2, :])[:, first * P:last * P]

        sems = {}

        def sem(name):
            sems[name] = ctx.enter_context(nc.semaphore(name))
            return sems[name]

        raw_loaded = [sem(f"raw_loaded{i}") for i in range(RING)]
        ada_loaded = [sem(f"ada_loaded{i}") for i in range(ADA_RING)]
        x_loaded = [sem(f"x_loaded{k}") for k in range(KT)]
        cols_loaded, square_loaded = sem("cols_loaded"), sem("square_loaded")
        lam_loaded, rope_loaded, out_stored = sem("lam_loaded"), sem("rope_loaded"), sem("out_stored")
        hi_done = sem("hi_done")
        lo_done = sem("lo_done")
        v_used = sem("v_used")
        job_done = sem("job_done")
        evac = sem("evac")
        aevac = sem("aevac")
        ghi = sem("ghi")
        g_ready = sem("g_ready")
        mset = sem("mset")
        halo = sem("halo")
        consts = sem("consts")
        c_act = sem("c_act")
        ada_used = sem("ada_used")
        cols_done = sem("cols_done")
        mod_done = sem("mod_done")
        scales = sem("scales")
        lam_done = sem("lam_done")
        lam_exp = sem("lam_exp")
        sq_done = sem("sq_done")
        ssum = sem("ssum")
        mean_done = sem("mean_done")
        root_done = sem("root_done")
        inv_done = sem("inv_done")
        spread_done = sem("spread_done")
        bcast_done = sem("bcast_done")
        xn_done = sem("xn_done")
        hh_done = sem("hh_done")
        h_ready = sem("h_ready")
        ct_done = sem("ct_done")
        csq_done, cmean_done, croot_done = sem("csq_done"), sem("cmean_done"), sem("croot_done")
        cinv_done, cspread_done, cbc_done = sem("cinv_done"), sem("cspread_done"), sem("cbc_done")
        cg_done = sem("cg_done")
        rraw = sem("rraw")
        shifted = sem("shifted")
        rcos, rsin = sem("rcos"), sem("rsin")
        rope_done = sem("rope_done")
        q_moved, k_moved = sem("q_moved"), sem("k_moved")
        score_done, masked, max_done = sem("score_done"), sem("masked"), sem("max_done")
        exp_done, rsum_done, ratio_done = sem("exp_done"), sem("rsum_done"), sem("ratio_done")
        diff_done = sem("diff_done")
        tr_done = sem("tr_done")
        dt_done = sem("dt_done")
        pv_done, o_done, osq_done = sem("pv_done"), sem("o_done"), sem("osq_done")
        oroot_done, oinv_done, onorm_done = sem("oroot_done"), sem("oinv_done"), sem("onorm_done")
        ot_done = sem("ot_done")

        block = ctx.enter_context(nc.Block())

        @block.sync
        def _(sp):
            sp.wait_ge(ada_used, KT)
            for n in range(RING):
                sp.dma_start(Wr[:, n, :], units[n]).then_inc(raw_loaded[n], 16)
            sp.dma_start(Rope[:], rope_d).then_inc(rope_loaded, 16)
            with sp.Fori(1, UNITS // RING) as i:
                for s in range(RING):
                    sp.wait_ge(lo_done, i * RING + (s - RING + 1))
                    sp.dma_start(Wr[:, s, :], units[i * RING + s]).then_inc(raw_loaded[s], 16)
            for n in range(UNITS // RING * RING, UNITS):
                sp.wait_ge(lo_done, n - RING + 1)
                sp.dma_start(Wr[:, n % RING, :], units[n]).then_inc(raw_loaded[n % RING], 16)
            for h in range(NH):
                for k in range(KT):
                    sp.wait_ge(hh_done, (6 + h) * KT + k + 1)
                    sp.dma_start(out_t[k, :, half(h)], Out[:, k, half(h)]).then_inc(out_stored, 16)
            sp.wait_ge(out_stored, 16 * NH * KT)

        @block.gpsimd
        def _(pool):
            for r in range(ADA_RING):
                pool.dma_start(Ada[:, r, :], ada[r]).then_inc(ada_loaded[r], 16)
            with pool.Fori(1, SECTIONS * KT // ADA_RING) as i:
                for s in range(ADA_RING):
                    pool.wait_ge(ada_used, i * ADA_RING + (s - ADA_RING + 1))
                    pool.dma_start(Ada[:, s, :], ada[i * ADA_RING + s]).then_inc(ada_loaded[s], 16)

            def rope(m, j, raw, other, to):
                at = m * 4 + j
                pool.wait_ge(rraw, at + 1)
                if not (isinstance(m, int) and m == 0 and j == 0):
                    pool.wait_ge(rope_done, at)
                nc.gpsimd.tensor_tensor(to, raw, Rope[:, 0, half(j % 2)], ALU.mult).then_inc(rcos, 1)
                for a in range(0, P, 32):
                    pool.dma_start(other[a:a + 32, :], raw[a ^ 32:(a ^ 32) + 32, :]).then_inc(shifted, 16)
                pool.wait_ge(shifted, at * 64 + 64)
                nc.gpsimd.tensor_tensor(other, other, Rope[:, 1, half(j % 2)], ALU.mult).then_inc(rsin, 1)
                pool.wait_ge(rcos, at + 1)
                pool.wait_ge(rsin, at + 1)
                nc.gpsimd.tensor_tensor(to, to, other, ALU.add).then_inc(rope_done, 1)

            pool.wait_ge(rope_loaded, 16)
            for j in range(4):
                rope(0, j, TmpA[:, j % 2, :], TmpG[:, j % 2, :], QK[:, j // 2, half(j % 2)])

            def body(hh, prev):
                for j in range(4):
                    if prev and j % 2 == 0:
                        pool.wait_ge(k_moved if j else q_moved, hh)
                    rope(hh + 1, j, TmpA[:, 0, :], TmpA[:, 1, :], (NextK if j >= 2 else NextQ)[:, half(j % 2)])

            body(0, False)
            with pool.Fori(1, HEADS - 1) as hh:
                body(hh, True)

        @block.scalar
        def _(act):
            def split_hi(n, wait, value, i=0, per=0):
                act.wait_ge(wait, value)
                act.wait_ge(raw_loaded[n % RING], 16 * (n // RING + 1) + i * (16 * per // RING))
                nc.scalar.activation(Wh[:, n % RING, :], Wr[:, n % RING, :], ACT.Copy).then_inc(hi_done, 1)

            def g_hi(slot, h, wait, value):
                act.wait_ge(wait, value)
                nc.scalar.activation(Gh[:, slot, half(h)], TmpG[:, h, :], ACT.Copy).then_inc(ghi, 1)

            def square(q, d):
                if d >= 3:
                    act.wait_ge(ssum, q * (KT - 1) + d - 2)
                out = Sq[:, d % 2, :] if d else SqSum[:, q % NH, :]
                nc.scalar.activation(out, X[:, d, half(q % NH)], ACT.Square).then_inc(sq_done, 1)

            def root(q):
                act.wait_ge(mean_done, q + 1)
                nc.scalar.activation(Root[:, 4 * (q % 2):4 * (q % 2) + 4], PS[:, 6, 0:4], ACT.Sqrt, bias=EpsC[:, 0:1]).then_inc(root_done, 1)

            def norm_chunk(q, k, shift, out=None, xn=None):
                at = q * KT + k
                act.wait_ge(xn_done, at + 1)
                if out is None and at >= 2:
                    act.wait_ge(h_ready, at - 1)
                outs = (TmpG[:, k % 2, :], Hh[:, k, half(q % NH)]) if out is None else (out[:, k, half(q % NH)],)
                for o in outs:
                    made = nc.scalar.activation(o, TmpA[:, k % 2, :] if xn is None else xn, ACT.Identity,
                                                bias=Mod[:, shift * KT + k:shift * KT + k + 1],
                                                scale=Scale[:, q // NH, k:k + 1])
                made.then_inc(hh_done, 1)

            def norm_tiles(q0, shift, split=(), jobs=0, out=None):
                for k in range(KT):
                    norm_chunk(q0, k, shift, out)
                    if k == 1:
                        for n in split[:1]:
                            split_hi(n, job_done, jobs)
                        root(q0 + 1)
                for n in split[1:]:
                    split_hi(n, job_done, jobs)
                for k in range(KT):
                    norm_chunk(q0 + 1, k, shift, out)

            def tail_squares(q0, e_end):
                for h in range(NH):
                    for d in range(KT):
                        act.wait_ge(evac, e_end - (NH - h) * KT + d + 1)
                        square(q0 + h, d)
                        if h and d == 3:
                            root(q0)

            def ffn_group(phase, g, n0, first=False, final=False):
                J, E = JOBS[phase] + g * 24, EVAC[phase] + g * 20
                if first:
                    act.wait_ge(hh_done, (NH if phase == "ffn1" else 3 * NH) * KT)
                else:
                    for c in (1, 2):
                        split_hi(n0 + c, job_done, J, g, 6)
                for f in range(GF):
                    for h in range(NH):
                        q = f * NH + h
                        act.wait_ge(job_done, J + 2 * q + 1)
                        if q >= 2:
                            act.wait_ge(evac, E + q - 1)
                        nc.scalar.activation(TmpA[:, h, :], PS[:, (2 * q) % BANKS, :], ACT.Silu).then_inc(aevac, 1)
                        if h == 1:
                            split_hi(n0 + 3 + 2 * f, job_done, J + 2 * q + 1, g, 6)
                        g_hi(f, h, evac, E + q + 1)
                    if not (final and f == GF - 1):
                        split_hi(n0 + 4 + 2 * f, job_done, J + 4 * f + 4, g, 6)

            act.dma_start(Cols[:], cols_d).then_inc(cols_loaded, 16)
            act.dma_start(Lam4[:], lam_d).then_inc(lam_loaded, 16)
            for k in range(KT):
                act.dma_start(X[:, k, :], x_t[k]).then_inc(x_loaded[k], 16)
                if k == 1:
                    act.dma_start(Square[:], square_d).then_inc(square_loaded, 16)
            act.wait_ge(cols_loaded, 16)
            nc.scalar.activation(CAct[:], col("c", 0, KT), ACT.Silu).then_inc(c_act, 1)
            act.wait_ge(lam_done, 2)
            nc.scalar.activation(LamS[:, 2:4], LamS[:, 0:2], ACT.Exp).then_inc(lam_exp, 1)
            act.wait_ge(consts, 1)
            for d in range(KT):
                act.wait_ge(x_loaded[d], 16)
                for h in range(NH):
                    if d >= 2:
                        act.wait_ge(ssum, NH * (d - 2) + h + 1)
                    out = Sq[:, h, :] if d else SqSum[:, h, :]
                    nc.scalar.activation(out, X[:, d, half(h)], ACT.Square).then_inc(sq_done, 1)
            for q in range(NH):
                root(q)
            for n in range(RING):
                act.wait_ge(raw_loaded[n], 16)
                nc.scalar.activation(Wh[:, n, :], Wr[:, n, :], ACT.Copy).then_inc(hi_done, 1)
            act.wait_ge(scales, 1)
            act.wait_ge(xn_done, NH * KT)
            for q in range(NH):
                for k in range(KT):
                    norm_chunk(q, k, SH1, xn=XN[:, k, half(q)])

            ffn_group("ffn1", 0, 0, first=True)
            with act.Fori(1, NG) as g:
                ffn_group("ffn1", g, 0)
            act.wait_ge(scales, 7)
            tail_squares(2, EVAC["conv"])
            norm_tiles(2, SH2, (U_CONV + 1, U_CONV + 2), JOBS["conv"])

            for cg in range(2):
                J, E, n0 = JOBS["conv"] + 28 * cg, EVAC["conv"] + 24 * cg, U_CONV + 8 * cg

                def copy_u(q):
                    act.wait_ge(job_done, J + 3 * q + 1)
                    if q >= 2:
                        act.wait_ge(evac, E + 2 * q - 3)
                    nc.scalar.activation(TmpA[:, q % 2, :], PS[:, (3 * q) % BANKS, :], ACT.Copy).then_inc(aevac, 1)

                if cg:
                    for c in (1, 2):
                        split_hi(n0 + c, job_done, J)
                else:
                    act.wait_ge(hh_done, 2 * NH * KT)
                copy_u(0)
                for q in range(4):
                    jt, h, cq = q // 2, q % 2, 4 * cg + q
                    if h == 1:
                        split_hi(n0 + 3 * jt + 3, job_done, J + 3 * q + 1)
                        split_hi(n0 + 3 * jt + 4, job_done, J + 3 * q + 2)
                    act.wait_ge(evac, E + 2 * q + 2)
                    nc.scalar.activation(Sq[:, h, :], CT[:, half(h)], ACT.Square).then_inc(csq_done, 1)
                    if h == 1:
                        split_hi(n0 + 3 * jt + 5, job_done, J + 3 * q + 3)
                    act.wait_ge(cmean_done, cq + 1)
                    nc.scalar.activation(Root[:, 0:8], PS[:, 6, 0:8], ACT.Sqrt, bias=EpsC[:, 0:1])\
                        .then_inc(croot_done, 1)
                    if q < 3:
                        copy_u(q + 1)
                    g_hi(jt, h, cg_done, cq + 1)

            def raw(m, j, bank, job, slot, free):
                act.wait_ge(job_done, job)
                if free is not None:
                    act.wait_ge(rope_done, free)
                nc.scalar.activation(TmpA[:, slot, :], PS[:, bank, :], ACT.Copy,
                                     scale=DH ** -0.5 if j < 2 else 1.0).then_inc(rraw, 1)

            for c in (1, 2):
                split_hi(U_Q0 + c, job_done, JOBS["v"])
            for j in range(4):
                raw(0, j, 4 + j, JOBS["v"] + j + 1, j % 2, j - 1 if j >= 2 else None)
                if j % 2:
                    split_hi(U_Q0 + 3 + j // 2, job_done, JOBS["v"] + j + 1)
            for c in (1, 2, 3):
                split_hi(U_V + 2 + c, v_used, c)
            for t in range(0, QB, 2):
                act.wait_ge(job_done, JOBS["v"] + 4 + t + 1)
                nc.scalar.activation(V[:, t, :], PS[:, t, :], ACT.Copy).then_inc(aevac, 1)

            def exps(i, at):
                for c in range(2):
                    act.wait_ge(max_done, at * 2 + c + 1)
                    nc.scalar.activation(PR[:, c, 0:P * (i + 1)], scores(c, 0, i + 1), ACT.Exp,
                                         bias=NMax[:, c:c + 1], accum_out=Sum[:, c:c + 1]).then_inc(exp_done, 1)

            def copy_o(i, at):
                act.wait_ge(pv_done, at + 1)
                nc.scalar.activation(O[:, i, :], PS[:, 5, 0:P], ACT.Copy, scale=RSum[:, i, 0:1]).then_inc(o_done, 1)

            def square_o(i, at):
                act.wait_ge(o_done, at + 1)
                if not (isinstance(at, int) and at == 0):
                    act.wait_ge(osq_done, at)
                nc.scalar.activation(Junk[:], O[:, i, :], ACT.Square, accum_out=SqO[:, i:i + 1]).then_inc(osq_done, 1)

            def root_o(at):
                act.wait_ge(osq_done, at)
                nc.scalar.activation(Root[:, 0:QB], SqO[:], ACT.Sqrt, bias=EpsC[:, 1:2], scale=1.0 / P)\
                    .then_inc(oroot_done, 1)

            def o_hi(h, bank, count):
                act.wait_ge(ot_done, count + h + 1)
                nc.scalar.activation(Gh[:, 0, half(h)], PS[:, bank, :], ACT.Copy, scale=SubG[:, 0:1]).then_inc(ghi, 1)

            def body(hh, nq, ny, prev, nxt):
                J = JOBS["att"] + (hh * 20 - 16 if prev else 0)
                i3, per = (hh, 3) if prev and nxt else (0, 0)
                for i in range(QB):
                    at = hh * QB + i
                    if i < QB - 1 or nxt:
                        exps((i + 1) % QB, at + 1)
                    if nxt and i in STEP_OF_JOB:
                        j = STEP_OF_JOB.index(i)
                        raw(hh + 1, j, 6 + j % 2, J + j + 1, 0, hh * 4 + 4 + j)
                        if j % 2:
                            split_hi(nq + 3 + j // 2, job_done, J + j + 1, i3, per)
                    if prev and i == 1:
                        for h in range(NH):
                            o_hi(h, (4 if nxt else 6) + h, hh * NH - NH)
                    if nxt and i == QB - 2:
                        act.wait_ge(rope_done, hh * 4 + 6)
                        act.wait_ge(score_done, hh * (2 * QB) + 2 * QB)
                        nc.scalar.activation(QK[:, 0, 0:S], NextQ[:], ACT.Copy).then_inc(q_moved, 1)
                    if i or prev:
                        copy_o((i - 1) % QB, at - 1)
                    if prev and i == 0:
                        square_o(QB - 1, at - 1)
                        root_o(at)
                    for r in range(ROUNDS[i]):
                        act.wait_ge(tr_done, hh * ALL_ROUNDS + DT_COUNT[i] - ROUNDS[i] + r + 1)
                        n = min(4, i + 1 - 4 * r)
                        nc.scalar.activation(DT[:, 4 * r * P:(4 * r + n) * P], PS[:, 4, 0:n * P], ACT.Copy)\
                            .then_inc(dt_done, 1)
                    if i:
                        square_o(i - 1, at - 1)
                if prev:
                    split_hi(ny + 3, job_done, J + (20 if nxt else 16), i3, per)

            exps(0, 0)
            split_hi(U_HEAD, job_done, JOBS["att"])
            body(0, U_Q1, None, False, True)
            with act.Fori(1, HEADS - 1) as hh:
                body(hh, U_HEAD - 3, U_HEAD - 1, True, True)
            body(HEADS - 1, None, U_WO2, True, False)
            copy_o(QB - 1, HEADS * QB - 1)
            square_o(QB - 1, HEADS * QB - 1)
            root_o(HEADS * QB)
            for h in range(NH):
                o_hi(h, 4 + h, (HEADS - 1) * NH)
            tail_squares(4, EVAC["ffn2"])
            norm_tiles(4, SH3, (U_FFN2 + 2,), JOBS["ffn2"])

            ffn_group("ffn2", 0, U_FFN2, first=True)
            with act.Fori(1, NG - 1) as g:
                ffn_group("ffn2", g, U_FFN2)
            ffn_group("ffn2", NG - 1, U_FFN2, final=True)
            tail_squares(6, EVAC["end"])
            norm_tiles(6, SHF, out=Out)

        @block.vector
        def _(dve):
            def split_lo(n, i=0, per=0):
                dve.wait_ge(hi_done, n + 1 + i * per)
                nc.vector.tensor_tensor(Wl[:, n % RING, :], Wr[:, n % RING, :], Wh[:, n % RING, :].bitcast(F32),
                                        ALU.subtract).then_inc(lo_done, 1)

            def g_lo(slot, h, count):
                dve.wait_ge(ghi, count)
                nc.vector.tensor_tensor(Gl[:, slot, half(h)], TmpG[:, h, :], Gh[:, slot, half(h)].bitcast(F32),
                                        ALU.subtract).then_inc(g_ready, 1)

            def ada_tile(s, k):
                dve.wait_ge(ada_loaded[k % ADA_RING], 16 * (s * (KT // ADA_RING) + k // ADA_RING + 1))
                w = Ada[:, k % ADA_RING, :]
                if k == 0:
                    if not (isinstance(s, int) and s == 0):
                        dve.wait_ge(cols_done, s)
                    nc.vector.tensor_scalar(AdaSum[:], w, CAct[:, 0:1], None, ALU.mult).then_inc(ada_used, 1)
                else:
                    dve.wait_ge(ada_used, s * KT + k)
                    nc.vector.scalar_tensor_tensor(AdaSum[:], w, CAct[:, k:k + 1], AdaSum[:], ALU.mult, ALU.add)\
                        .then_inc(ada_used, 1)

            def ada_bias(s):
                dve.wait_ge(cols_done, s + 1)
                nc.vector.tensor_tensor(Mod[:, bass.ts(s, KT)], PS[:, 7, 0:KT], Cols[:, bass.ts(s, KT)], ALU.add)\
                    .then_inc(mod_done, 1)

            def scale(n, section, gain):
                dve.wait_ge(mod_done, section + 1)
                nc.vector.scalar_tensor_tensor(Scale[:, n, :], Mod[:, bass.ts(section, KT)], 1.0, col(gain, 0, KT),
                                               ALU.add, ALU.mult).then_inc(scales, 1)

            def gate(n, section, factor):
                dve.wait_ge(mod_done, section + 1)
                nc.vector.tensor_scalar(Gate[:, n, :], Mod[:, bass.ts(section, KT)], factor, None, ALU.mult)\
                    .then_inc(scales, 1)

            def add_squares(q, d):
                dve.wait_ge(sq_done, q * KT + d + 1)
                if d >= 2:
                    dve.wait_ge(ssum, q * (KT - 1) + d - 1)
                nc.vector.tensor_tensor(SqSum[:, q % NH, :], SqSum[:, q % NH, :], Sq[:, d % 2, :], ALU.add)\
                    .then_inc(ssum, 1)

            def spread(q):
                dve.wait_ge(root_done, q + 1)
                part = slice(4 * (q % 2), 4 * (q % 2) + 4)
                nc.vector.reciprocal(Inv[:, part], Root[:, part]).then_inc(inv_done, 1)
                dve.wait_ge(inv_done, q + 1)
                nc.vector.tensor_copy(Spread[:, q % NH, :].rearrange("p (b c) -> p b c", b=4),
                                      Inv[:, part].unsqueeze(2).to_broadcast([P, 4, P])).then_inc(spread_done, 1)

            def norm_mul(q, k):
                at = q * KT + k
                if k == 0:
                    dve.wait_ge(bcast_done, q + 1)
                if at >= 2:
                    dve.wait_ge(hh_done, at - 1)
                nc.vector.tensor_tensor(TmpA[:, k % 2, :], X[:, k, half(q % NH)], PS[:, 7 - q % 2, :], ALU.mult)\
                    .then_inc(xn_done, 1)

            def norm_lo(q, k):
                dve.wait_ge(hh_done, q * KT + k + 1)
                nc.vector.tensor_tensor(Hl[:, k, half(q % NH)], TmpG[:, k % 2, :],
                                        Hh[:, k, half(q % NH)].bitcast(F32), ALU.subtract).then_inc(h_ready, 1)

            def norm_tiles(q0, split=(), final=False):
                for q in (q0, q0 + 1):
                    for k in range(KT):
                        norm_mul(q, k)
                        if k and not final:
                            norm_lo(q, k - 1)
                        if q == q0 and k == 2:
                            for n in split[:1]:
                                split_lo(n)
                        if q == q0 and k == 3:
                            spread(q0 + 1)
                    if not final:
                        norm_lo(q, KT - 1)
                    if q == q0:
                        for n in split[1:]:
                            split_lo(n)

            def add_out(job, n, t, bank):
                h, d = t // KT, t % KT
                dve.wait_ge(job_done, job + t + 1)
                nc.vector.scalar_tensor_tensor(X[:, d, half(h)], PS[:, bank, :], Gate[:, n, d:d + 1],
                                               X[:, d, half(h)], ALU.mult, ALU.add).then_inc(evac, 1)

            def add_outs(job, n, q0=None):
                for t in range(NH * KT):
                    add_out(job, n, t, (job_bank + t) % BANKS)
                    if q0 is None:
                        continue
                    q, d = q0 + t // KT, t % KT
                    if d >= 2:
                        add_squares(q, d - 1)
                    if d == KT - 1:
                        add_squares(q, d)
                    if t == KT + 5:
                        spread(q0)

            def ffn_group(phase, g, n0, n, first=False, final=False, ada=False, q0=None):
                nonlocal job_bank
                J, G, A = JOBS[phase] + g * 24, GDONE[phase] + g * 4, AEVAC[phase] + g * 4
                if first:
                    dve.wait_ge(h_ready, (NH if phase == "ffn1" else 3 * NH) * KT)
                else:
                    for c in (1, 2):
                        split_lo(n0 + c, g, 6)
                for f in range(GF):
                    for h in range(NH):
                        q = f * NH + h
                        if ada:
                            ada_tile(g + 2, 2 * q)
                            ada_tile(g + 2, 2 * q + 1)
                        if h == 1:
                            split_lo(n0 + 3 + 2 * f, g, 6)
                        dve.wait_ge(job_done, J + 2 * q + 2)
                        dve.wait_ge(aevac, A + q + 1)
                        nc.vector.tensor_tensor(TmpG[:, h, :], TmpA[:, h, :], PS[:, (2 * q + 1) % BANKS, :], ALU.mult)\
                            .then_inc(evac, 1)
                        g_lo(f, h, G + q + 1)
                    if not (final and f == GF - 1):
                        split_lo(n0 + 4 + 2 * f, g, 6)
                if ada:
                    ada_bias(g + 2)
                if first and n == 0:
                    gate(0, GT1, 0.5)
                    dve.wait_ge(scales, 2)
                job_bank = 8
                add_outs(J + 8, n, q0)

            job_bank = 0
            nc.vector.memset(Ones[:], 1.0)
            nc.vector.memset(Mean[:], 1.0 / D)
            nc.vector.memset(MeanG[:], 0.0).then_inc(mset, 1)
            nc.vector.memset(EpsC[:, 1:2], SUB_EPS)
            dve.wait_ge(mset, 1)
            for gi in range(2):
                nc.vector.memset(MeanG[gi * DH:(gi + 1) * DH, gi:gi + 1], 1.0 / DH)
            nc.vector.memset(EpsC[:, 0:1], EPS).then_inc(consts, 1)
            dve.wait_ge(lam_loaded, 16)
            nc.vector.tensor_tensor(LamP[:], Lam4[:, 0:2, :], Lam4[:, 2:4, :], ALU.mult).then_inc(lam_done, 1)
            dve.wait_ge(lam_done, 1)
            nc.vector.tensor_reduce(LamS[:, 0:2], LamP[:], AX.X, ALU.add).then_inc(lam_done, 1)
            dve.wait_ge(c_act, 1)
            for k in range(KT):
                ada_tile(SH1, k)
                for h in range(NH if k else 0):
                    dve.wait_ge(sq_done, NH * k + h + 1)
                    if k > 1:
                        dve.wait_ge(ssum, NH * (k - 2) + h + 1)
                    nc.vector.tensor_tensor(SqSum[:, h, :], SqSum[:, h, :], Sq[:, h, :], ALU.add).then_inc(ssum, 1)
            dve.wait_ge(lam_exp, 1)
            nc.vector.tensor_tensor(LamS[:, 4:5], LamS[:, 3:4], LamS[:, 2:3], ALU.subtract).then_inc(lam_done, 1)
            dve.wait_ge(lam_done, 3)
            nc.vector.tensor_scalar(LamS[:, 5:6], LamS[:, 4:5], -LAMBDA_INIT, None, ALU.add).then_inc(lam_done, 1)
            nc.vector.tensor_scalar(SubG[:], col("subln"), 1.0 - LAMBDA_INIT, None, ALU.mult).then_inc(lam_done, 1)
            ada_bias(SH1)
            for q in range(NH):
                spread(q)
            for k in range(KT):
                ada_tile(SC1, k)
                if k == 0:
                    dve.wait_ge(bcast_done, NH)
                for h in range(NH):
                    nc.vector.tensor_tensor(XN[:, k, half(h)], X[:, k, half(h)], PS[:, 7 - h, :], ALU.mult)\
                        .then_inc(xn_done, 1)
            ada_bias(SC1)
            scale(0, SC1, "g1")
            for n in range(RING - 1):
                split_lo(n)
            for q in range(NH):
                for k in range(KT):
                    norm_lo(q, k)
                    if q == 0 and k == KT - 1:
                        split_lo(RING - 1)

            ffn_group("ffn1", 0, 0, 0, first=True, ada=True)
            with dve.Fori(1, SECTIONS - 2) as g:
                ffn_group("ffn1", g, 0, 0, ada=True)
            for n, section, gain in ((1, SC2, "g2"), (2, SC3, "g3"), (3, SCF, "gf")):
                scale(n, section, gain)
            gate(1, GT2, 1.0)
            gate(2, GT3, 0.5)
            dve.wait_ge(scales, 7)
            ffn_group("ffn1", NG - 2, 0, 0)
            ffn_group("ffn1", NG - 1, 0, 0, q0=2)
            norm_tiles(2, (U_CONV + 1, U_CONV + 2))

            nc.vector.memset(CU[:, 0:2], 0.0).then_inc(halo, 1)
            dve.wait_ge(halo, 1)
            for cg in range(2):
                J, E, A, G = JOBS["conv"] + 28 * cg, EVAC["conv"] + 24 * cg, AEVAC["conv"] + 4 * cg, GDONE["conv"] + 4 * cg
                n0 = U_CONV + 8 * cg
                if cg:
                    for c in (1, 2):
                        split_lo(n0 + c)
                for q in range(4):
                    jt, h, cq = q // 2, q % 2, 4 * cg + q
                    tile = 2 * cg + jt
                    dve.wait_ge(job_done, J + 3 * q + 2)
                    dve.wait_ge(aevac, A + q + 1)
                    nc.vector.tensor_tensor(CU[:, 2 + h * HALF:2 + (h + 1) * HALF], TmpA[:, h, :],
                                            PS[:, (3 * q + 1) % BANKS, :], ALU.mult).then_inc(evac, 1)
                    dve.wait_ge(evac, E + 2 * q + 1)
                    nc.vector.tensor_scalar(CT[:, half(h)], CU[:, 2 + h * HALF:2 + (h + 1) * HALF],
                                            col("conv_w", 2 * 4 + tile), None, ALU.mult).then_inc(ct_done, 1)
                    for tap in (1, 0):
                        dve.wait_ge(ct_done, cq * 3 + 2 - tap)
                        nc.vector.scalar_tensor_tensor(CT[:, half(h)], CU[:, tap + h * HALF:tap + (h + 1) * HALF],
                                                       col("conv_w", tap * 4 + tile), CT[:, half(h)],
                                                       ALU.mult, ALU.add).then_inc(ct_done, 1)
                    if h == 1:
                        split_lo(n0 + 3 * jt + 3)
                        split_lo(n0 + 3 * jt + 4)
                    dve.wait_ge(job_done, J + 3 * q + 3)
                    dve.wait_ge(ct_done, cq * 3 + 3)
                    nc.vector.tensor_tensor(CT[:, half(h)], CT[:, half(h)], PS[:, (3 * q + 2) % BANKS, :], ALU.mult)\
                        .then_inc(evac, 1)
                    if h == 1:
                        split_lo(n0 + 3 * jt + 5)
                    dve.wait_ge(croot_done, cq + 1)
                    nc.vector.reciprocal(Inv[:, 0:8], Root[:, 0:8]).then_inc(cinv_done, 1)
                    dve.wait_ge(cinv_done, cq + 1)
                    nc.vector.tensor_copy(Spread[:, h, :].rearrange("p (b c) -> p b c", b=8),
                                          Inv[:, 0:8].unsqueeze(2).to_broadcast([P, 8, DH])).then_inc(cspread_done, 1)
                    dve.wait_ge(cbc_done, cq + 1)
                    nc.vector.scalar_tensor_tensor(TmpG[:, h, :], CT[:, half(h)], col("conv_g", tile), PS[:, 7, :],
                                                   ALU.mult, ALU.mult).then_inc(cg_done, 1)
                    g_lo(jt, h, G + q + 1)
                job_bank = 12
                add_outs(J + 12, 1)

            for c in range(1, 8):
                split_lo(U_Q0 + c)
            for t in range(1, QB, 2):
                dve.wait_ge(job_done, JOBS["v"] + 4 + t + 1)
                nc.vector.tensor_copy(V[:, t, :], PS[:, t, :]).then_inc(evac, 1)

            def maxima(i, at):
                for c in range(2):
                    dve.wait_ge(score_done, at * 2 + c + 1)
                    nc.vector.tensor_tensor(scores(c, i, i + 1), scores(c, i, i + 1), mask, ALU.add).then_inc(masked, 1)
                    dve.wait_ge(masked, at * 2 + c + 1)
                    nc.vector.tensor_reduce(NMax[:, c:c + 1], scores(c, 0, i + 1), AX.X, ALU.max, negate=True)\
                        .then_inc(max_done, 1)

            def difference(i, at, rounds):
                w = P * (i + 1)
                dve.wait_ge(exp_done, at * 2 + 2)
                nc.vector.reciprocal(RSum[:, i, :], Sum[:]).then_inc(rsum_done, 1)
                dve.wait_ge(rsum_done, at + 1)
                nc.vector.scalar_tensor_tensor(Ratio[:], RSum[:, i, 1:2], LamS[:, 5:6], Sum[:, 0:1], ALU.mult, ALU.mult)\
                    .then_inc(ratio_done, 1)
                dve.wait_ge(ratio_done, at + 1)
                if rounds is not None:
                    dve.wait_ge(tr_done, rounds)
                nc.vector.scalar_tensor_tensor(PR[:, 2, 0:w], PR[:, 1, 0:w], Ratio[:, 0:1], PR[:, 0, 0:w],
                                               ALU.mult, ALU.add).then_inc(diff_done, 1)

            def norm_o(count):
                dve.wait_ge(oroot_done, count)
                nc.vector.reciprocal(Inv[:, 0:QB], Root[:, 0:QB]).then_inc(oinv_done, 1)
                dve.wait_ge(oinv_done, count)
                nc.vector.tensor_tensor(O[:], O[:], Inv[:, 0:QB].unsqueeze(2).to_broadcast([P, QB, P]), ALU.mult)\
                    .then_inc(onorm_done, 1)

            def o_lo(h, bank, count):
                dve.wait_ge(ghi, count + h + 1)
                nc.vector.scalar_tensor_tensor(Gl[:, 0, half(h)], PS[:, bank, :], SubG[:, 0:1],
                                               Gh[:, 0, half(h)].bitcast(F32), ALU.mult, ALU.subtract).then_inc(g_ready, 1)

            def body(hh, nq, ny, prev, nxt):
                nonlocal job_bank
                J = JOBS["att"] + (hh * 20 - 16 if prev else 0)
                i3, per = (hh, 3) if prev and nxt else (0, 0)
                tile = 0
                for i in range(QB):
                    at = hh * QB + i
                    difference(i, at, hh * ALL_ROUNDS + (DT_COUNT[i - 1] if i else 0) if i or prev else None)
                    if i < QB - 1 or nxt:
                        maxima((i + 1) % QB, at + 1)
                    if prev and i == 0:
                        norm_o(hh)
                    if prev and i == 1:
                        for h in range(NH):
                            o_lo(h, (4 if nxt else 6) + h, GDONE["att"] + hh * NH - NH)
                    if nxt and i in STEP_OF_JOB and STEP_OF_JOB.index(i) % 2:
                        split_lo(nq + 3 + STEP_OF_JOB.index(i) // 2, i3, per)
                    if nxt and i == QB - 2:
                        dve.wait_ge(rope_done, hh * 4 + 8)
                        dve.wait_ge(score_done, hh * (2 * QB) + 2 * QB)
                        nc.vector.tensor_copy(QK[:, 1, 0:S], NextK[:]).then_inc(k_moved, 1)
                    for _ in range((TILES if nxt else TILES_LAST)[i] if prev else 0):
                        add_out(J + (4 if nxt else 0), 1, tile, 6 + tile % 2)
                        tile += 1
                if prev:
                    split_lo(ny + 3, i3, per)

            maxima(0, 0)
            split_lo(U_HEAD)
            body(0, U_Q1, None, False, True)
            with dve.Fori(1, HEADS - 1) as hh:
                body(hh, U_HEAD - 3, U_HEAD - 1, True, True)
            body(HEADS - 1, None, U_WO2, True, False)
            norm_o(HEADS)
            for h in range(NH):
                o_lo(h, 4 + h, GDONE["att"] + (HEADS - 1) * NH)
            job_bank = 0
            add_outs(JOBS["ffn2"] - 16, 1, 4)
            norm_tiles(4, (U_FFN2 + 2,))

            ffn_group("ffn2", 0, U_FFN2, 2, first=True)
            with dve.Fori(1, NG - 1) as g:
                ffn_group("ffn2", g, U_FFN2, 2)
            ffn_group("ffn2", NG - 1, U_FFN2, 2, final=True, q0=6)
            norm_tiles(6, final=True)

        @block.tensor
        def _(pe):
            def mm(out, lhs, rhs, first, last):
                return nc.tensor.matmul(out, lhs, rhs, start=first, stop=last)

            def products(bank, n, h, ks):
                for k in ks:
                    s, w = n % RING, blk(k)
                    mm(PS[:, bank, :], Wh[:, s, w], Hh[:, k, half(h)], k == 0, False)
                    mm(PS[:, bank, :], Wh[:, s, w], Hl[:, k, half(h)], False, False)
                    made = mm(PS[:, bank, :], Wl[:, s, w], Hh[:, k, half(h)], False, k == KT - 1)
                    if k == KT - 1:
                        made.then_inc(job_done, 1)

            def project(bank, n, h):
                products(bank, n, h, range(KT))

            LAG = 3

            def project_new(bank, n, h, q):
                for k in range(KT + LAG):
                    if k < KT:
                        pe.wait_ge(h_ready, q * KT + k + 1)
                        products(bank, n, h, (k,))
                    if k >= LAG:
                        if k == LAG:
                            pe.wait_ge(lo_done, n + 2)
                        products(bank + 1, n + 1, h, (k - LAG,))
                    if k == 4 and q % 2 == 0 and q:
                        bcast(q + 1)

            def out_job(bank, ns, t):
                h, d = t // KT, t % KT
                for f, n in enumerate(ns):
                    s, w = n % RING, blk(d)
                    mm(PS[:, bank, :], Wh[:, s, w], Gh[:, f, half(h)], f == 0, False)
                    mm(PS[:, bank, :], Wh[:, s, w], Gl[:, f, half(h)], False, False)
                    made = mm(PS[:, bank, :], Wl[:, s, w], Gh[:, f, half(h)], False, f == len(ns) - 1)
                made.then_inc(job_done, 1)

            def mean(q):
                pe.wait_ge(ssum, (q + 1) * (KT - 1) if q >= NH else NH * (KT - 1))
                for b in range(4):
                    made = mm(PS[:, 6, b:b + 1], SqSum[:, q % NH, blk(b)], Mean[:], True, True)
                made.then_inc(mean_done, 1)

            def bcast(q):
                pe.wait_ge(spread_done, q + 1)
                for b in range(4):
                    made = mm(PS[:, 7 - q % 2, blk(b)], Spread[:, q % NH, blk(b)], ident, True, True)
                made.then_inc(bcast_done, 1)

            def ada_cols(s):
                pe.wait_ge(ada_used, s * KT + KT)
                for c in range(KT):
                    made = mm(PS[:, 7, c:c + 1], AdaSum[:, blk(c)], Ones[:], True, True)
                made.then_inc(cols_done, 1)

            def norm_between(q0, t):
                if q0 is not None and t == KT + 2:
                    mean(q0)
                if q0 is not None and t == KT + 6:
                    bcast(q0)

            def ffn_group(phase, g, n0, first=False, ada=False, q=None, q0=None):
                J, E, A, G = JOBS[phase] + g * 24, EVAC[phase] + g * 20, AEVAC[phase] + g * 4, GDONE[phase] + g * 4

                def bank_free(L):
                    if L < BANKS:
                        if not first:
                            pe.wait_ge(evac, E - 5 + L)
                        elif EVAC[phase]:
                            pe.wait_ge(evac, E)
                    elif L < BANKS + 8:
                        pe.wait_ge(*((evac, E + (L - BANKS) // 2 + 1) if L % 2 else (aevac, A + (L - BANKS) // 2 + 1)))
                    else:
                        pe.wait_ge(evac, E + 4 + L - 14 + 1)

                for f in range(GF):
                    for h in range(NH):
                        for w in range(2):
                            L = 4 * f + 2 * h + w
                            bank_free(L)
                            if q is not None and f == 0:
                                if w == 0:
                                    pe.wait_ge(lo_done, n0 + 1)
                                    bank_free(L + 1)
                                    project_new(L, n0, h, q + h)
                                continue
                            if h == 0:
                                pe.wait_ge(lo_done, n0 + 2 * f + w + 1 + g * 6)
                            project(L % BANKS, n0 + 2 * f + w, h)
                if ada:
                    ada_cols(g + 2)
                pe.wait_ge(lo_done, n0 + 6 + g * 6)
                for t in range(NH * KT):
                    bank_free(8 + t)
                    if t % KT == 0:
                        pe.wait_ge(g_ready, G + 3 + t // KT)
                    out_job((8 + t) % BANKS, (n0 + 4, n0 + 5), t)
                    norm_between(q0, t)
                if q0 is not None:
                    mean(q0 + 1)

            pe.wait_ge(consts, 1)
            ada_cols(SH1)
            pe.wait_ge(square_loaded, 16)
            pe.wait_ge(mod_done, 1)
            mean(0)
            pe.wait_ge(root_done, 1)
            mean(1)
            bcast(0)
            bcast(1)
            pe.wait_ge(xn_done, NH * KT)
            ada_cols(SC1)
            ffn_group("ffn1", 0, 0, first=True, ada=True, q=0)
            with pe.Fori(1, SECTIONS - 2) as g:
                ffn_group("ffn1", g, 0, ada=True)
            ffn_group("ffn1", NG - 2, 0)
            ffn_group("ffn1", NG - 1, 0, q0=2)

            for cg in range(2):
                J, E, A, G = JOBS["conv"] + 28 * cg, EVAC["conv"] + 24 * cg, AEVAC["conv"] + 4 * cg, GDONE["conv"] + 4 * cg
                n0 = U_CONV + 8 * cg

                def reader(L):
                    q, w = L // 3, L % 3
                    if L >= 12:
                        return evac, E + 8 + L - 12 + 1
                    return (evac, E + 2 * q + w) if w else (aevac, A + q + 1)

                def group_mean(q):
                    pe.wait_ge(csq_done, 4 * cg + q + 1)
                    for b in range(4):
                        made = mm(PS[:, 6, 2 * b:2 * b + 2], Sq[:, q % 2, blk(b)], MeanG[:], True, True)
                    made.then_inc(cmean_done, 1)

                def group_bcast(q):
                    pe.wait_ge(cspread_done, 4 * cg + q + 1)
                    for b in range(4):
                        made = mm(PS[:, 7, blk(b)], Spread[:, q % 2, blk(b)], ident, True, True)
                    made.then_inc(cbc_done, 1)

                for L in range(12):
                    q, w = L // 3, L % 3
                    if L < BANKS:
                        pe.wait_ge(evac, E)
                    else:
                        pe.wait_ge(*reader(L - BANKS))
                    if cg == 0 and q < 2 and w < 2:
                        if w == 0:
                            pe.wait_ge(lo_done, n0 + 1)
                            project_new(L, n0, q, 2 + q)
                    else:
                        if q % 2 == 0:
                            pe.wait_ge(lo_done, n0 + 3 * (q // 2) + w + 1)
                        project(L % BANKS, n0 + 3 * (q // 2) + w, q % 2)
                    if q and w == 0:
                        group_mean(q - 1)
                    if q and w == 1:
                        group_bcast(q - 1)
                pe.wait_ge(lo_done, n0 + 8)
                for t in range(NH * KT):
                    pe.wait_ge(*reader(12 + t - BANKS))
                    if t % KT == 0:
                        pe.wait_ge(g_ready, G + 3 + t // KT)
                    out_job((12 + t) % BANKS, (n0 + 6, n0 + 7), t)
                    if t == 1:
                        group_mean(3)
                    if t == 4:
                        group_bcast(3)

            for j in range(4):
                if j < 2:
                    pe.wait_ge(evac, EVAC["v"] - (4 if j == 0 else 0))
                if j % 2 == 0:
                    pe.wait_ge(lo_done, U_Q0 + j // 2 + 1)
                project(4 + j, U_Q0 + j // 2, j % 2)

            for u in range(4):
                pe.wait_ge(lo_done, U_V + u + 1)
                s = (U_V + u) % RING
                for kk in range(2):
                    k, w = 2 * u + kk, half(kk)
                    for t in range(QB):
                        if k == 0 and t >= 4:
                            pe.wait_ge(rraw, t - 3)
                        mm(PS[:, t, :], Hh[:, k, blk(t)], Wh[:, s, w], k == 0, False)
                        mm(PS[:, t, :], Hl[:, k, blk(t)], Wh[:, s, w], False, False)
                        made = mm(PS[:, t, :], Hh[:, k, blk(t)], Wl[:, s, w], False, k == KT - 1)
                        if k == KT - 1:
                            made.then_inc(job_done, 1)
                if u < 3:
                    made.then_inc(v_used, 1)

            def score(i, at):
                for c in range(2):
                    if not (isinstance(at, int) and at == 0):
                        pe.wait_ge(exp_done, at * 2 - 1 + c)
                    part = slice(c * DH, (c + 1) * DH)
                    for a in range(0, P * (i + 1), HALF):
                        b = min(a + HALF, P * (i + 1))
                        made = mm(PS[:, 2 * c + a // HALF, 0:b - a], QK[part, 0, blk(i)], QK[part, 1, a:b], True, True)
                    made.then_inc(score_done, 1)

            def values(i, hh):
                pe.wait_ge(dt_done, hh * ALL_ROUNDS + DT_COUNT[i])
                if i:
                    pe.wait_ge(o_done, hh * QB + i)
                for b in range(i + 1):
                    made = mm(PS[:, 5, 0:P], DT[:, blk(b)], V[:, b, bass.ts(hh, P)], b == 0, b == i)
                made.then_inc(pv_done, 1)

            def turn_o(banks, count):
                pe.wait_ge(onorm_done, count)
                for i in range(QB):
                    made = nc.tensor.transpose(PS[:, banks + i // 4, blk(i % 4)], O[:, i, :], ident)
                    if i % 4 == 3:
                        made.then_inc(ot_done, 1)

            def body(hh, nq, ny, prev, nxt):
                E, G = EVAC["att"] + hh * 16 - 16, GDONE["att"] + hh * NH - NH
                per = 3 if prev and nxt else 0
                chunk, tile = 0, 0

                def chunks(n):
                    nonlocal chunk
                    for _ in range(n):
                        j, k = chunk // KT, chunk % KT
                        if k == 0:
                            if j < 2 and j == 0:
                                pe.wait_ge(rraw, hh * 4 + 4)
                                if prev:
                                    pe.wait_ge(evac, E)
                            elif j >= 2:
                                pe.wait_ge(rraw, hh * 4 + 4 + j - 1)
                            if j % 2 == 0:
                                pe.wait_ge(lo_done, nq + j // 2 + 1 + (hh * per if per else 0))
                        products(6 + j % 2, nq + j // 2, j % 2, (k,))
                        chunk += 1

                def tiles(n):
                    nonlocal tile
                    for _ in range(n):
                        t = tile
                        if t == 0:
                            pe.wait_ge(lo_done, ny + 1 + (hh * per if per else 0))
                            if nxt:
                                pe.wait_ge(rraw, hh * 4 + 8)
                        if t % KT == 0:
                            pe.wait_ge(g_ready, G + (t // KT + 1 if nxt else NH))
                        if t >= 2:
                            pe.wait_ge(evac, E + t - 1)
                        out_job(6 + t % 2, (ny,), t)
                        tile += 1

                for i in range(QB):
                    at = hh * QB + i
                    if i < QB - 1 or nxt:
                        if i == QB - 1:
                            pe.wait_ge(q_moved, hh + 1)
                            pe.wait_ge(k_moved, hh + 1)
                        score((i + 1) % QB, at + 1)
                    n = CHUNKS[i] if nxt else 0
                    if prev and i == 1:
                        chunks(n // 2)
                        if nxt:
                            pe.wait_ge(dt_done, hh * ALL_ROUNDS + 1)
                        turn_o(4 if nxt else 6, hh)
                        n -= n // 2
                    late = 2 if n and i >= 4 else 0
                    chunks(n - late)
                    n = (TILES if nxt else TILES_LAST)[i] if prev else 0
                    split = [min(2, n), int(n > 2), int(n > 3), max(n - 4, 0)]
                    tiles(split[0])
                    if i:
                        if i == 1 and prev and nxt:
                            pe.wait_ge(g_ready, G + NH)
                        values(i - 1, hh)
                    elif prev:
                        values(QB - 1, hh - 1)
                    tiles(split[1])
                    pe.wait_ge(diff_done, at + 1)
                    for r in range(ROUNDS[i]):
                        before = DT_COUNT[i] - ROUNDS[i] + r
                        if before or prev:
                            pe.wait_ge(dt_done, hh * ALL_ROUNDS + before)
                        for b in range(4 * r, min(4 * r + 4, i + 1)):
                            made = nc.tensor.transpose(PS[:, 4, blk(b % 4)], PR[:, 2, blk(b)], ident)
                        made.then_inc(tr_done, 1)
                        if r == 0:
                            tiles(split[2])
                            chunks(late)
                    tiles(split[3])

            pe.wait_ge(rope_done, 4)
            pe.wait_ge(aevac, AEVAC["att"])
            pe.wait_ge(evac, EVAC["att"])
            score(0, 0)
            body(0, U_Q1, None, False, True)
            with pe.Fori(1, HEADS - 1) as hh:
                body(hh, U_HEAD - 3, U_HEAD - 1, True, True)
            body(HEADS - 1, None, U_WO2, True, False)
            values(QB - 1, HEADS - 1)
            turn_o(4, HEADS)
            pe.wait_ge(lo_done, U_WO2 + 2)
            for t in range(NH * KT):
                if t % KT == 0:
                    pe.wait_ge(g_ready, GDONE["ffn2"] - NH + t // KT + 1)
                if t == 4:
                    pe.wait_ge(g_ready, GDONE["ffn2"])
                if t >= BANKS:
                    pe.wait_ge(evac, EVAC["ffn2"] - 16 + t - BANKS + 1)
                out_job(t % BANKS, (U_WO2 + 1,), t)
                norm_between(4, t)
            mean(5)

            ffn_group("ffn2", 0, U_FFN2, first=True, q=4)
            with pe.Fori(1, NG - 1) as g:
                ffn_group("ffn2", g, U_FFN2)
            ffn_group("ffn2", NG - 1, U_FFN2, q0=6)
            bcast(7)


def kernel(**inputs):
    import numpy as np
    import concourse.bacc as bacc
    from concourse.bass_utils import run_bass_kernel_spmd

    a = {k: np.asarray(v) for k, v in inputs.items()}

    def cols(w, at):
        return w[:, at:at + P].reshape(KT, P, P).transpose(1, 0, 2).reshape(P, D)

    def rows(w, n):
        return w[n * P:(n + 1) * P]

    w_in, w_out = a["w_in"][0], a["w_out"][0]
    width = HEADS * P
    V0, B0, C0, U0 = 2 * width, 3 * width, 4 * width, 5 * width
    units = []

    def ffn_units(w1, w3, w2):
        for g in range(NG):
            for f in range(GF * g, GF * g + GF):
                units.extend([cols(w1, f * P), cols(w3, f * P)])
            units.extend(rows(w2, f) for f in range(GF * g, GF * g + GF))

    ffn_units(a["ffn1_w1"][0], a["ffn1_w3"][0], a["ffn1_w2"][0])
    for cg in range(2):
        for t in (2 * cg, 2 * cg + 1):
            units.extend(cols(w_in, at + t * P) for at in (U0, C0, B0))
        units.extend(rows(w_out, HEADS + t) for t in (2 * cg, 2 * cg + 1))
    def qk_units(h):
        return [cols(w_in, h * P), cols(w_in, width + h * P)]

    units.extend(qk_units(0))
    for u in range(4):
        units.append(w_in[2 * u * P:(2 * u + 2) * P, V0:V0 + width].reshape(2, P, width).transpose(1, 0, 2).reshape(P, D))
    units.extend(qk_units(1))
    for h in range(2):
        units.extend(qk_units(h + 2) + [rows(w_out, h)])
    units.extend([rows(w_out, 2), rows(w_out, 3)])
    ffn_units(a["ffn2_w1"][0], a["ffn2_w3"][0], a["ffn2_w2"][0])

    ada_w = np.concatenate([a["w_ada"][0], a["w_ada_final"]], axis=1)
    ada_b = np.concatenate([a["b_ada"][0], a["b_ada_final"]])

    def down(v):
        return v.reshape(-1, P).T

    inv = (1.0 / (np.float32(10000.0) ** (np.arange(0, DH, 2, dtype=np.float32) / np.float32(DH)))).astype(np.float32)
    ang = (np.arange(S, dtype=np.float32)[:, None] * inv[None, :]).astype(np.float32)
    cos, sin = np.cos(ang).T, np.sin(ang).T
    rope = np.stack([np.concatenate([cos] * 4), np.concatenate([-sin, sin] * 2)], axis=1)
    below = np.where(np.arange(P)[None, :] <= np.arange(P)[:, None], 0.0, MASKED)
    arrays = {
        "units": np.stack(units),
        "ada": ada_w.reshape(KT, P, SECTIONS, D).transpose(2, 0, 1, 3).reshape(SECTIONS * KT, P, D),
        "x_t": a["x"][0].T.reshape(KT, P, S),
        "cols": np.concatenate([down(ada_b), down(a["c"][0]), down(a["g_ffn1"][0]), down(a["g_mix"][0]),
                                down(a["g_ffn2"][0]), down(a["g_final"]), down(a["subln_g"][0]),
                                down(a["conv_w"][0].reshape(-1)), down(a["conv_norm_g"][0])], axis=1),
        "lam": np.broadcast_to(np.stack([a["lambda_q1"][0], a["lambda_q2"][0], a["lambda_k1"][0],
                                         a["lambda_k2"][0]])[None], (P, 4, DH)),
        "rope": rope.astype(np.float32),
        "square": np.stack([np.eye(P), below], axis=1).astype(np.float32),
    }
    arrays = {k: np.ascontiguousarray(v) for k, v in arrays.items()}
    nc = bacc.Bacc("TRN2", target_bir_lowering=False, num_devices=1)
    aps = [nc.dram_tensor(k, v.shape, mybir.dt.from_np(v.dtype), kind="ExternalInput").ap() for k, v in arrays.items()]
    out_t = nc.dram_tensor("out_t", (KT, P, S), F32, kind="ExternalOutput").ap()
    program(nc, *aps, out_t)
    got = run_bass_kernel_spmd(nc, [arrays], core_ids=[0])
    return np.ascontiguousarray(got.results[0]["out_t"].reshape(D, S).T)[None]
```

```python
from contextlib import ExitStack

import concourse.bass as bass
from concourse import mybir

F32 = mybir.dt.float32
F32R = mybir.dt.float32r
ALU = mybir.AluOpType
ACT = mybir.ActivationFunctionType
AX = mybir.AxisListType

P = 128
D = 1024
S = 1024
KT = D // P
HALF = 512
NH = S // HALF
F = 2816
FT = F // P
GF = 2
NG = FT // GF
HEADS = 4
DH = 64
QB = S // P
EPS = 1e-6
SUB_EPS = 1e-5
LAMBDA_INIT = 0.8 - 0.6
MASKED = -3.0e38

RING = 3
ADA_RING = 4
BANKS = 6
SECTIONS = 11
SH1, SC1, GT1, SH2, SC2, GT2, SH3, SC3, GT3, SHF, SCF = range(SECTIONS)

U_FFN = NG * 3 * GF
U_CONV = U_FFN
U_Q0 = U_CONV + 16
U_V = U_Q0 + 2
U_Q1 = U_V + 4
U_HEAD = U_Q1 + 2
U_WO2 = U_HEAD + 6
U_FFN2 = U_WO2 + 2
UNITS = U_FFN2 + U_FFN

JOBS = {"ffn1": 0}
EVAC = {"ffn1": 0}
AEVAC = {"ffn1": 0}
GDONE = {"ffn1": 0}
for _now, _next, _n, _j, _e, _a, _g in (("ffn1", "conv", NG, 24, 20, 4, 4), ("conv", "v", 2, 28, 24, 4, 4),
                                        ("v", "att", 1, 12, 4, 4, 0), ("att", "ffn2", HEADS, 19, 16, 0, 2),
                                        ("ffn2", "end", NG, 24, 20, 4, 4)):
    JOBS[_next] = JOBS[_now] + _n * _j
    EVAC[_next] = EVAC[_now] + _n * _e
    AEVAC[_next] = AEVAC[_now] + _n * _a
    GDONE[_next] = GDONE[_now] + _n * _g

CHUNKS = (7, 7, 6, 6, 6, 0, 0, 0)
CHUNKS_FIRST = (6, 6, 5, 5, 5, 5, 0, 0)
TILES = (0, 0, 0, 0, 0, 5, 6, 5)
TILES_LAST = (0, 0, 2, 2, 2, 3, 2, 0, 5)
FIRST = 3
assert sum(CHUNKS) == 2 * NH * KT and sum(TILES) == sum(TILES_LAST) == NH * KT
STEP_OF_JOB, STEP_OF_JOB_FIRST = [
    [next(i for i in range(QB) if sum(c[:i + 1]) >= KT * (j + 1)) for j in range(4)] for c in (CHUNKS, CHUNKS_FIRST)]
ROUNDS = [b // 4 + 1 for b in range(QB)]
DT_COUNT = [sum(ROUNDS[:b + 1]) for b in range(QB)]
ALL_ROUNDS = DT_COUNT[-1]

EARLY = {2: 2, 4: 0, 6: 2}

COLS = {}
_at = 0
for _name, _n in (("b_ada", SECTIONS * KT), ("c", KT), ("g1", KT), ("g2", KT), ("g3", KT), ("gf", KT),
                  ("subln", 1), ("conv_w", 12), ("conv_g", 4)):
    COLS[_name] = (_at, _n)
    _at += _n
NCOLS = _at


def program(nc, units, ada, x_t, cols_d, lam_d, rope_d, square_d, out_t):
    ctx = ExitStack()
    with ctx:
        at = [16512]

        def place(name, shape, dtype=F32, like=None):
            size = 4
            for n in shape[1:]:
                size *= n
            offset = at[0] if like is None else like
            if like is None:
                at[0] += (size + 31) // 32 * 32
            return nc.alloc_sbuf_tensor_at(name, shape, dtype, offset=offset), offset

        X, _ = place("X", [P, KT, S])
        Hh, h_at = place("Hh", [P, KT, S], F32R)
        Hl, hl_at = place("Hl", [P, KT, S], F32R)
        Wr, _ = place("Wr", [P, RING, S])
        Wh, _ = place("Wh", [P, RING, S], F32R)
        Wl, _ = place("Wl", [P, RING, S], F32R)
        Gh, gh_at = place("Gh", [P, GF, S], F32R)
        Gl, gl_at = place("Gl", [P, GF, S], F32R)
        NextQ, _ = place("NextQ", [P, S], like=gh_at + 4 * S)
        NextK, _ = place("NextK", [P, S], like=gl_at + 4 * S)
        V, v_at = place("V", [P, QB, HEADS * P])
        Ada, _ = place("Ada", [P, ADA_RING, D], like=v_at)
        QK, qk_at = place("QK", [P, 2, S + 8])
        AdaSum, _ = place("AdaSum", [P, D], like=qk_at)
        CU, _ = place("CU", [P, S + 2], like=qk_at)
        CT, _ = place("CT", [P, S], like=qk_at + 4 * (S + 8))
        PR, pr_at = place("PR", [P, 3, S])
        SqSum, _ = place("SqSum", [P, NH, HALF], like=pr_at)
        Sq, _ = place("Sq", [P, 2, HALF], like=pr_at + 4 * S)
        Spread, _ = place("Spread", [P, NH, HALF], like=pr_at + 8 * S)
        Rope, _ = place("Rope", [P, 2, S])
        TmpA, tmp_at = place("TmpA", [P, 2, HALF])
        TmpG, _ = place("TmpG", [P, 2, HALF])
        AdaRow, _ = place("AdaRow", [P, D], like=tmp_at + 4 * S)
        DT, _ = place("DT", [P, S], like=tmp_at + 4 * S)
        Lam4, _ = place("Lam4", [P, 4, DH], like=tmp_at)
        O, o_at = place("O", [P, QB, P])
        LamP, _ = place("LamP", [P, 2, DH], like=o_at)
        Square, _ = place("Square", [P, 2, P])
        Cols, _ = place("Cols", [P, NCOLS])
        Mod, _ = place("Mod", [P, SECTIONS * KT])
        Scale, _ = place("Scale", [P, 4, KT])
        Gate, _ = place("Gate", [P, 3, KT])
        CAct, _ = place("CAct", [P, KT])
        Ones, _ = place("Ones", [P, 1])
        Mean, _ = place("Mean", [P, 1])
        MeanG, _ = place("MeanG", [P, 2])
        EpsC, _ = place("EpsC", [P, 2])
        Root, _ = place("Root", [P, 8])
        Inv, _ = place("Inv", [P, 8])
        LamS, _ = place("LamS", [P, 8])
        SubG, _ = place("SubG", [P, 1])
        NMax, _ = place("NMax", [P, 2])
        Sum, _ = place("Sum", [P, 2])
        RSum, _ = place("RSum", [P, QB, 2])
        Ratio, _ = place("Ratio", [P, 1])
        Junk, _ = place("Junk", [P, P])
        SqO, _ = place("SqO", [P, QB])
        Out, _ = place("Out", [P, KT, S], like=h_at)
        AdaFirst, _ = place("AdaFirst", [P, KT, D], like=h_at)
        XN, _ = place("XN", [P, KT, S], like=hl_at)
        assert at[0] <= nc.sbuf_usable_end

        PS = nc.alloc_psum_tensor("PS", [P, 8, HALF], F32)
        ident, mask = Square[:, 0, :], Square[:, 1, :]

        def col(name, i=0, n=1):
            a = COLS[name][0] + i
            return Cols[:, a:a + n]

        def half(h):
            return slice(h * HALF, (h + 1) * HALF)

        def blk(b):
            return slice(b * P, (b + 1) * P)

        def flat(ap):
            return ap.rearrange("p a b -> p (a b)")

        def scores(c, first, last):
            return flat(PS[:, 2 * c:2 * c + 2, :])[:, first * P:last * P]

        sems = {}

        def sem(name):
            sems[name] = ctx.enter_context(nc.semaphore(name))
            return sems[name]

        raw_loaded = [sem(f"raw_loaded{i}") for i in range(RING)]
        ada_loaded = [sem(f"ada_loaded{i}") for i in range(ADA_RING)]
        first_loaded = [sem(f"first_loaded{k}") for k in range(KT)]
        x_loaded = [sem(f"x_loaded{k}") for k in range(KT)]
        cols_loaded, square_loaded = sem("cols_loaded"), sem("square_loaded")
        lam_loaded, rope_loaded, out_stored = sem("lam_loaded"), sem("rope_loaded"), sem("out_stored")
        hi_done = sem("hi_done")
        lo_done = sem("lo_done")
        v_used = sem("v_used")
        job_done = sem("job_done")
        evac = sem("evac")
        aevac = sem("aevac")
        ghi = sem("ghi")
        g_ready = sem("g_ready")
        mset = sem("mset")
        halo = sem("halo")
        consts = sem("consts")
        c_act = sem("c_act")
        ada_used = sem("ada_used")
        row_used = sem("row_used")
        row_done = sem("row_done")
        hf_done = sem("hf_done")
        cols_done = sem("cols_done")
        mod_done = sem("mod_done")
        scales = sem("scales")
        lam_done = sem("lam_done")
        lam_exp = sem("lam_exp")
        sq_done = sem("sq_done")
        ssum = sem("ssum")
        mean_done = sem("mean_done")
        root_done = sem("root_done")
        inv_done = sem("inv_done")
        spread_done = sem("spread_done")
        bcast_done = sem("bcast_done")
        xn_done = sem("xn_done")
        hh_done = sem("hh_done")
        h_ready = sem("h_ready")
        ct_done = sem("ct_done")
        csq_done, cmean_done, croot_done = sem("csq_done"), sem("cmean_done"), sem("croot_done")
        cinv_done, cspread_done, cbc_done = sem("cinv_done"), sem("cspread_done"), sem("cbc_done")
        cg_done = sem("cg_done")
        rraw = sem("rraw")
        shifted = [sem(f"shifted{i}") for i in range(2)]
        rcos, rsin = sem("rcos"), sem("rsin")
        rope_done = sem("rope_done")
        q_moved, k_moved = sem("q_moved"), sem("k_moved")
        score_done, masked, max_done = sem("score_done"), sem("masked"), sem("max_done")
        exp_done, rsum_done, ratio_done = sem("exp_done"), sem("rsum_done"), sem("ratio_done")
        diff_done = sem("diff_done")
        tr_done = sem("tr_done")
        dt_done = sem("dt_done")
        pv_done, o_done, osq_done = sem("pv_done"), sem("o_done"), sem("osq_done")
        oroot_done, oinv_done, onorm_done = sem("oroot_done"), sem("oinv_done"), sem("onorm_done")
        ot_done = sem("ot_done")

        block = ctx.enter_context(nc.Block())

        @block.sync
        def _(sp):
            for n in range(RING):
                sp.wait_ge(ada_used, (1, 2, KT)[n])
                sp.dma_start(Wr[:, n, :], units[n]).then_inc(raw_loaded[n], 16)
            sp.dma_start(Rope[:], rope_d).then_inc(rope_loaded, 16)
            with sp.Fori(1, UNITS // RING) as i:
                for s in range(RING):
                    sp.wait_ge(lo_done, i * RING + (s - RING + 1))
                    sp.dma_start(Wr[:, s, :], units[i * RING + s]).then_inc(raw_loaded[s], 16)
            for n in range(UNITS // RING * RING, UNITS):
                sp.wait_ge(lo_done, n - RING + 1)
                sp.dma_start(Wr[:, n % RING, :], units[n]).then_inc(raw_loaded[n % RING], 16)
            for h in range(NH):
                for k in range(KT):
                    sp.wait_ge(hh_done, (6 + h) * KT + k + 1)
                    sp.dma_start(out_t[k, :, half(h)], Out[:, k, half(h)]).then_inc(out_stored, 16)
            sp.wait_ge(out_stored, 16 * NH * KT)

        @block.gpsimd
        def _(pool):
            for k in range(KT):
                pool.dma_start(AdaFirst[:, k, :], ada[k]).then_inc(first_loaded[k], 16)
            for r in range(ADA_RING):
                pool.dma_start(Ada[:, r, :], ada[KT + r]).then_inc(ada_loaded[r], 16)
            with pool.Fori(KT // ADA_RING + 1, SECTIONS * KT // ADA_RING) as i:
                for s in range(ADA_RING):
                    pool.wait_ge(ada_used, i * ADA_RING + (s - ADA_RING + 1 - KT))
                    pool.dma_start(Ada[:, s, :], ada[i * ADA_RING + s]).then_inc(ada_loaded[s], 16)

            def rope(m, j, raw, other, to):
                at = m * 4 + j
                pool.wait_ge(rraw, at + 1)
                nc.gpsimd.tensor_tensor(to, raw, Rope[:, 0, half(j % 2)], ALU.mult).then_inc(rcos, 1)
                pool.wait_ge(shifted[j % 2], m * 128 + 64 * (j // 2 + 1))
                nc.gpsimd.tensor_tensor(other, other, Rope[:, 1, half(j % 2)], ALU.mult).then_inc(rsin, 1)
                pool.wait_ge(rcos, at + 1)
                pool.wait_ge(rsin, at + 1)
                nc.gpsimd.tensor_tensor(to, to, other, ALU.add).then_inc(rope_done, 1)

            def body(hh, prev):
                for j in range(4):
                    if prev and j % 2 == 0:
                        pool.wait_ge(k_moved if j else q_moved, hh)
                    rope(hh + 1, j, TmpA[:, 0, :], TmpA[:, 1, :], (NextK if j >= 2 else NextQ)[:, half(j % 2)])

            def add_squares(q):
                for d in range(1, KT):
                    pool.wait_ge(sq_done, q * KT + d + 1)
                    pool.wait_ge(ssum, q * (KT - 1) + d - 1)
                    nc.gpsimd.tensor_tensor(SqSum[:, q % NH, :], SqSum[:, q % NH, :], Sq[:, d % 2, :], ALU.add)\
                        .then_inc(ssum, 1)

            add_squares(3)
            pool.wait_ge(rope_loaded, 16)
            for j in range(4):
                rope(0, j, TmpA[:, j % 2, :], TmpG[:, j % 2, :], QK[:, j // 2, half(j % 2)])
            body(0, False)
            with pool.Fori(1, HEADS - 1) as hh:
                body(hh, True)
            add_squares(7)

        @block.scalar
        def _(act):
            def split_hi(n, wait, value, i=0, per=0):
                act.wait_ge(wait, value)
                act.wait_ge(raw_loaded[n % RING], 16 * (n // RING + 1) + i * (16 * per // RING))
                nc.scalar.activation(Wh[:, n % RING, :], Wr[:, n % RING, :], ACT.Copy).then_inc(hi_done, 1)

            def g_hi(slot, h, wait, value):
                act.wait_ge(wait, value)
                nc.scalar.activation(Gh[:, slot, half(h)], TmpG[:, h, :], ACT.Copy).then_inc(ghi, 1)

            def square(q, d):
                if d >= 3 or (d and q % NH and EARLY[q - 1]):
                    before = d - 2 if d >= 3 else 1 - d
                    act.wait_ge(ssum, q * (KT - 1) + before)
                out = Sq[:, d % 2, :] if d else SqSum[:, q % NH, :]
                nc.scalar.activation(out, X[:, d, half(q % NH)], ACT.Square).then_inc(sq_done, 1)

            def root(q):
                act.wait_ge(mean_done, q + 1)
                nc.scalar.activation(Root[:, 4 * (q % 2):4 * (q % 2) + 4], PS[:, 6, 0:4], ACT.Sqrt, bias=EpsC[:, 0:1]).then_inc(root_done, 1)

            def norm_chunk(q, k, shift, out=None):
                at = q * KT + k
                act.wait_ge(xn_done, at + 1)
                if out is None and at >= 2:
                    act.wait_ge(h_ready, at - 1)
                outs = (TmpG[:, k % 2, :], Hh[:, k, half(q % NH)]) if out is None else (out[:, k, half(q % NH)],)
                for o in outs:
                    made = nc.scalar.activation(o, TmpA[:, k % 2, :], ACT.Identity,
                                                bias=Mod[:, shift * KT + k:shift * KT + k + 1],
                                                scale=Scale[:, q // NH, k:k + 1])
                made.then_inc(hh_done, 1)

            def norm_tiles(q0, shift, split=(), jobs=0, out=None):
                early = EARLY[q0]
                for k in range(KT):
                    if k >= early:
                        norm_chunk(q0, k, shift, out)
                    if k == max(early, 1):
                        for n in split[:1]:
                            split_hi(n, job_done, jobs)
                    if k == (4 if early else 1):
                        root(q0 + 1)
                for n in split[1:]:
                    split_hi(n, job_done, jobs)
                for k in range(KT):
                    norm_chunk(q0 + 1, k, shift, out)

            def tail_squares(q0, e_end, root_at, shift, out=None):
                early = EARLY[q0]
                for t in range(NH * KT):
                    act.wait_ge(evac, e_end - NH * KT + t + 1)
                    square(q0 + t // KT, t % KT)
                    if t == root_at:
                        root(q0)
                    if NH * KT - 1 - early <= t < NH * KT - 1:
                        norm_chunk(q0, t - (NH * KT - 1 - early), shift, out)

            def ffn_group(phase, g, n0, first=False, final=False):
                J, E = JOBS[phase] + g * 24, EVAC[phase] + g * 20
                if first:
                    act.wait_ge(hh_done, (NH if phase == "ffn1" else 3 * NH) * KT)
                else:
                    for c in (1, 2):
                        split_hi(n0 + c, job_done, J, g, 6)
                for f in range(GF):
                    for h in range(NH):
                        q = f * NH + h
                        act.wait_ge(job_done, J + 2 * q + 1)
                        if q >= 2:
                            act.wait_ge(evac, E + q - 1)
                        nc.scalar.activation(TmpA[:, h, :], PS[:, (2 * q) % BANKS, :], ACT.Silu).then_inc(aevac, 1)
                        if h == 1:
                            split_hi(n0 + 3 + 2 * f, job_done, J + 2 * q + 1, g, 6)
                        g_hi(f, h, evac, E + q + 1)
                    if not (final and f == GF - 1):
                        split_hi(n0 + 4 + 2 * f, job_done, J + 4 * f + 4, g, 6)

            def first_hi(q, k):
                act.wait_ge(xn_done, q * KT + k + 1)
                nc.scalar.activation(Hh[:, k, half(q)], XN[:, k, half(q)], ACT.Identity,
                                     bias=Mod[:, SH1 * KT + k:SH1 * KT + k + 1], scale=Scale[:, 0, k:k + 1])\
                    .then_inc(hh_done, 1)

            act.dma_start(Cols[:], cols_d).then_inc(cols_loaded, 16)
            act.dma_start(Lam4[:], lam_d).then_inc(lam_loaded, 16)
            for k in range(KT):
                act.dma_start(X[:, k, :], x_t[k]).then_inc(x_loaded[k], 16)
                if k == 1:
                    act.dma_start(Square[:], square_d).then_inc(square_loaded, 16)
            act.wait_ge(cols_loaded, 16)
            nc.scalar.activation(CAct[:], col("c", 0, KT), ACT.Silu).then_inc(c_act, 1)
            act.wait_ge(lam_done, 2)
            nc.scalar.activation(LamS[:, 2:4], LamS[:, 0:2], ACT.Exp).then_inc(lam_exp, 1)
            act.wait_ge(consts, 1)
            for d in range(KT):
                act.wait_ge(x_loaded[d], 16)
                for h in range(NH):
                    if d >= 2:
                        act.wait_ge(ssum, NH * (d - 2) + h + 1)
                    out = Sq[:, h, :] if d else SqSum[:, h, :]
                    nc.scalar.activation(out, X[:, d, half(h)], ACT.Square).then_inc(sq_done, 1)
            for q in range(NH):
                root(q)
            act.wait_ge(row_used, KT)
            nc.scalar.activation(AdaRow[0:1, :], flat(PS[0:1, 0:2, :]), ACT.Copy).then_inc(row_done, 1)
            for n in range(RING):
                if n == RING - 1:
                    act.wait_ge(scales, 1)
                    for k in range(KT):
                        first_hi(0, k)
                act.wait_ge(raw_loaded[n], 16)
                nc.scalar.activation(Wh[:, n, :], Wr[:, n, :], ACT.Copy).then_inc(hi_done, 1)
            for k in range(KT):
                first_hi(1, k)

            ffn_group("ffn1", 0, 0, first=True)
            with act.Fori(1, NG) as g:
                ffn_group("ffn1", g, 0)
            act.wait_ge(scales, 7)
            tail_squares(2, EVAC["conv"], KT + 1, SH2)
            norm_tiles(2, SH2, (U_CONV + 1, U_CONV + 2), JOBS["conv"])

            for cg in range(2):
                J, E, n0 = JOBS["conv"] + 28 * cg, EVAC["conv"] + 24 * cg, U_CONV + 8 * cg

                def copy_u(q):
                    act.wait_ge(job_done, J + 3 * q + 1)
                    if q >= 2:
                        act.wait_ge(evac, E + 2 * q - 3)
                    nc.scalar.activation(TmpA[:, q % 2, :], PS[:, (3 * q) % BANKS, :], ACT.Copy).then_inc(aevac, 1)

                if cg:
                    for c in (1, 2):
                        split_hi(n0 + c, job_done, J)
                else:
                    act.wait_ge(hh_done, 2 * NH * KT)
                copy_u(0)
                for q in range(4):
                    jt, h, cq = q // 2, q % 2, 4 * cg + q
                    if h == 1:
                        split_hi(n0 + 3 * jt + 4, job_done, J + 3 * q + 2)
                    act.wait_ge(evac, E + 2 * q + 2)
                    nc.scalar.activation(Sq[:, h, :], CT[:, half(h)], ACT.Square).then_inc(csq_done, 1)
                    if h == 1:
                        split_hi(n0 + 3 * jt + 5, job_done, J + 3 * q + 3)
                    act.wait_ge(cmean_done, cq + 1)
                    nc.scalar.activation(Root[:, 0:8], PS[:, 6, 0:8], ACT.Sqrt, bias=EpsC[:, 0:1])\
                        .then_inc(croot_done, 1)
                    if q < 3:
                        copy_u(q + 1)
                    if h == 0:
                        split_hi(n0 + 3 * jt + 3, job_done, J + 3 * q + 4)
                    g_hi(jt, h, cg_done, cq + 1)

            def raw(m, j, bank, job, slot, back):
                act.wait_ge(job_done, job)
                if back == 1 or j >= 2:
                    act.wait_ge(rcos, m * 4 + j - back + 1)
                    act.wait_ge(shifted[(j - back) % 2], m * 128 + 64 * ((j - back) // 2 + 1))
                nc.scalar.activation(TmpA[:, slot, :], PS[:, bank, :], ACT.Copy,
                                     scale=DH ** -0.5 if j < 2 else 1.0).then_inc(rraw, 1)

            def exchange(j, slot, to):
                for a in range(0, P, 32):
                    act.dma_start(to[a:a + 32, :], TmpA[a ^ 32:(a ^ 32) + 32, slot, :]).then_inc(shifted[j % 2], 16)

            for c in (1, 2):
                split_hi(U_Q0 + c, job_done, JOBS["v"])
            for j in range(4):
                raw(0, j, 4 + j, JOBS["v"] + j + 1, j % 2, 2)
                act.wait_ge(rraw, j + 1)
                if j >= 2:
                    act.wait_ge(rope_done, j - 1)
                exchange(j, j % 2, TmpG[:, j % 2, :])
                if j % 2:
                    split_hi(U_Q0 + 3 + j // 2, job_done, JOBS["v"] + j + 1)
            for c in (1, 2, 3):
                split_hi(U_V + 2 + c, v_used, c)
            for t in range(0, QB, 2):
                act.wait_ge(job_done, JOBS["v"] + 4 + t + 1)
                nc.scalar.activation(V[:, t, :], PS[:, t, :], ACT.Copy).then_inc(aevac, 1)

            def exps(i, at):
                for c in range(2):
                    act.wait_ge(max_done, at * 2 + c + 1)
                    nc.scalar.activation(PR[:, c, 0:P * (i + 1)], scores(c, 0, i + 1), ACT.Exp,
                                         bias=NMax[:, c:c + 1], accum_out=Sum[:, c:c + 1]).then_inc(exp_done, 1)

            def copy_o(i, at):
                act.wait_ge(pv_done, at + 1)
                nc.scalar.activation(O[:, i, :], PS[:, 5, 0:P], ACT.Copy, scale=RSum[:, i, 0:1]).then_inc(o_done, 1)

            def square_o(i, at):
                act.wait_ge(o_done, at + 1)
                if not (isinstance(at, int) and at == 0):
                    act.wait_ge(osq_done, at)
                nc.scalar.activation(Junk[:], O[:, i, :], ACT.Square, accum_out=SqO[:, i:i + 1]).then_inc(osq_done, 1)

            def root_o(at):
                act.wait_ge(osq_done, at)
                nc.scalar.activation(Root[:, 0:QB], SqO[:], ACT.Sqrt, bias=EpsC[:, 1:2], scale=1.0 / P)\
                    .then_inc(oroot_done, 1)

            def o_hi(h, bank, count):
                act.wait_ge(ot_done, count + h + 1)
                nc.scalar.activation(Gh[:, 0, half(h)], PS[:, bank, :], ACT.Copy, scale=SubG[:, 0:1]).then_inc(ghi, 1)

            def body(hh, nq, ny, prev, nxt):
                J = JOBS["att"] + (hh * 20 - 16 if prev else 0)
                i3, per = (hh, 3) if prev and nxt else (0, 0)
                steps = STEP_OF_JOB if prev else STEP_OF_JOB_FIRST
                for i in range(QB):
                    at = hh * QB + i
                    if i == 0 and not nxt:
                        copy_o(QB - 1, at - 1)
                        square_o(QB - 1, at - 1)
                    if i != 1 and (i < QB - 1 or nxt):
                        exps((i + 1) % QB, at + 1)
                    if nxt and i in steps:
                        j = steps.index(i)
                        raw(hh + 1, j, 6 + j % 2, J + j + 1, 0, 1)
                    if prev and i == 1:
                        for h in range(NH):
                            o_hi(h, (4 if nxt else 6) + h, hh * NH - NH)
                    if i == 1:
                        exps(i + 1, at + 1)
                    if nxt and i == QB - 2:
                        act.wait_ge(rope_done, hh * 4 + 6)
                        act.wait_ge(score_done, hh * (2 * QB) + 2 * QB)
                        nc.scalar.activation(QK[:, 0, 0:S], NextQ[:], ACT.Copy).then_inc(q_moved, 1)
                    if i:
                        copy_o(i - 1, at - 1)
                    if prev and i == 0:
                        if nxt:
                            copy_o(QB - 1, at - 1)
                            square_o(QB - 1, at - 1)
                        root_o(at)
                    for r in range(ROUNDS[i]):
                        act.wait_ge(tr_done, hh * ALL_ROUNDS + DT_COUNT[i] - ROUNDS[i] + r + 1)
                        n = min(4, i + 1 - 4 * r)
                        nc.scalar.activation(DT[:, 4 * r * P:(4 * r + n) * P], PS[:, 4, 0:n * P], ACT.Copy)\
                            .then_inc(dt_done, 1)
                    rotated = nxt and i in steps
                    if rotated:
                        act.wait_ge(rraw, hh * 4 + 4 + j + 1)
                        act.wait_ge(rope_done, hh * 4 + 4 + j)
                    if i:
                        square_o(i - 1, at - 1)
                    if rotated:
                        exchange(j, 0, TmpA[:, 1, :])
                    if rotated and j % 2:
                        split_hi(nq + 3 + j // 2, job_done, J + j + 1, i3, per)
                if prev and nxt:
                    split_hi(ny + 3, job_done, J + 20, i3, per)

            exps(0, 0)
            split_hi(U_HEAD, job_done, JOBS["att"])
            body(0, U_Q1, None, False, True)
            with act.Fori(1, HEADS - 1) as hh:
                body(hh, U_HEAD - 3, U_HEAD - 1, True, True)
            body(HEADS - 1, None, U_WO2, True, False)
            copy_o(QB - 1, HEADS * QB - 1)
            square_o(QB - 1, HEADS * QB - 1)
            root_o(HEADS * QB)
            split_hi(U_WO2 + 3, job_done, JOBS["ffn2"] - 16)
            for h in range(NH):
                o_hi(h, 4 + h, (HEADS - 1) * NH)
            tail_squares(4, EVAC["ffn2"], KT + 3, SH3)
            norm_tiles(4, SH3, (U_FFN2 + 2,), JOBS["ffn2"])

            ffn_group("ffn2", 0, U_FFN2, first=True)
            with act.Fori(1, NG - 1) as g:
                ffn_group("ffn2", g, U_FFN2)
            ffn_group("ffn2", NG - 1, U_FFN2, final=True)
            tail_squares(6, EVAC["end"], KT + 1, SHF, Out)
            norm_tiles(6, SHF, out=Out)

        @block.vector
        def _(dve):
            def split_lo(n, i=0, per=0):
                dve.wait_ge(hi_done, n + 1 + i * per)
                nc.vector.tensor_tensor(Wl[:, n % RING, :], Wr[:, n % RING, :], Wh[:, n % RING, :].bitcast(F32),
                                        ALU.subtract).then_inc(lo_done, 1)

            def g_lo(slot, h, count):
                dve.wait_ge(ghi, count)
                nc.vector.tensor_tensor(Gl[:, slot, half(h)], TmpG[:, h, :], Gh[:, slot, half(h)].bitcast(F32),
                                        ALU.subtract).then_inc(g_ready, 1)

            def ada_tile(s, k):
                dve.wait_ge(ada_loaded[k % ADA_RING], 16 * ((s - 1) * (KT // ADA_RING) + k // ADA_RING + 1))
                w = Ada[:, k % ADA_RING, :]
                if k == 0:
                    if not (isinstance(s, int) and s == 1):
                        dve.wait_ge(cols_done, s)
                    nc.vector.tensor_scalar(AdaSum[:], w, CAct[:, 0:1], None, ALU.mult).then_inc(ada_used, 1)
                else:
                    dve.wait_ge(ada_used, (s - 1) * KT + k)
                    nc.vector.scalar_tensor_tensor(AdaSum[:], w, CAct[:, k:k + 1], AdaSum[:], ALU.mult, ALU.add)\
                        .then_inc(ada_used, 1)

            def ada_bias(s, bank=7):
                dve.wait_ge(cols_done, s + 1)
                nc.vector.tensor_tensor(Mod[:, bass.ts(s, KT)], PS[:, bank, 0:KT], Cols[:, bass.ts(s, KT)], ALU.add)\
                    .then_inc(mod_done, 1)

            def scale(n, section, gain):
                dve.wait_ge(mod_done, section + 1)
                nc.vector.scalar_tensor_tensor(Scale[:, n, :], Mod[:, bass.ts(section, KT)], 1.0, col(gain, 0, KT),
                                               ALU.add, ALU.mult).then_inc(scales, 1)

            def gate(n, section, factor):
                dve.wait_ge(mod_done, section + 1)
                nc.vector.tensor_scalar(Gate[:, n, :], Mod[:, bass.ts(section, KT)], factor, None, ALU.mult)\
                    .then_inc(scales, 1)

            def add_squares(q, d):
                dve.wait_ge(sq_done, q * KT + d + 1)
                if d >= 2:
                    dve.wait_ge(ssum, q * (KT - 1) + d - 1)
                nc.vector.tensor_tensor(SqSum[:, q % NH, :], SqSum[:, q % NH, :], Sq[:, d % 2, :], ALU.add)\
                    .then_inc(ssum, 1)

            def spread(q):
                dve.wait_ge(root_done, q + 1)
                part = slice(4 * (q % 2), 4 * (q % 2) + 4)
                nc.vector.reciprocal(Inv[:, part], Root[:, part]).then_inc(inv_done, 1)
                dve.wait_ge(inv_done, q + 1)
                nc.vector.tensor_copy(Spread[:, q % NH, :].rearrange("p (b c) -> p b c", b=4),
                                      Inv[:, part].unsqueeze(2).to_broadcast([P, 4, P])).then_inc(spread_done, 1)

            def norm_mul(q, k):
                at = q * KT + k
                if k == 0:
                    dve.wait_ge(bcast_done, q + 1)
                if at >= 2:
                    dve.wait_ge(hh_done, at - 1)
                nc.vector.tensor_tensor(TmpA[:, k % 2, :], X[:, k, half(q % NH)], PS[:, 7 - q % 2, :], ALU.mult)\
                    .then_inc(xn_done, 1)

            def norm_lo(q, k):
                dve.wait_ge(hh_done, q * KT + k + 1)
                nc.vector.tensor_tensor(Hl[:, k, half(q % NH)], TmpG[:, k % 2, :],
                                        Hh[:, k, half(q % NH)].bitcast(F32), ALU.subtract).then_inc(h_ready, 1)

            def norm_tiles(q0, split=(), final=False):
                early = EARLY[q0]
                for q in (q0, q0 + 1):
                    for k in range(KT):
                        if q > q0 or k >= early:
                            norm_mul(q, k)
                        if k and not final:
                            norm_lo(q, k - 1)
                        if q == q0 and k == max(early + 1, 2):
                            for n in split[:1]:
                                split_lo(n)
                        if q == q0 and k == (6 if early else 3):
                            spread(q0 + 1)
                    if not final:
                        norm_lo(q, KT - 1)
                    if q == q0:
                        for n in split[1:]:
                            split_lo(n)

            def add_out(job, n, t, bank):
                h, d = t // KT, t % KT
                dve.wait_ge(job_done, job + t + 1)
                nc.vector.scalar_tensor_tensor(X[:, d, half(h)], PS[:, bank, :], Gate[:, n, d:d + 1],
                                               X[:, d, half(h)], ALU.mult, ALU.add).then_inc(evac, 1)

            def add_outs(job, n, q0=None):
                for t in range(NH * KT):
                    add_out(job, n, t, (job_bank + t) % BANKS)
                    if q0 is None:
                        continue
                    early, d = EARLY[q0], t % KT
                    if t < KT or not early:
                        if d >= 2:
                            add_squares(q0 + t // KT, d - 1)
                        if d == KT - 1:
                            add_squares(q0 + t // KT, d)
                    if t == KT + (3 if early else 5):
                        spread(q0)
                    if NH * KT - 1 - early <= t < NH * KT - 1:
                        norm_mul(q0, t - (NH * KT - 1 - early))

            def ffn_group(phase, g, n0, n, first=False, final=False, ada=False, q0=None):
                nonlocal job_bank
                J, G, A = JOBS[phase] + g * 24, GDONE[phase] + g * 4, AEVAC[phase] + g * 4
                if first:
                    dve.wait_ge(h_ready, (NH if phase == "ffn1" else 3 * NH) * KT)
                else:
                    for c in (1, 2):
                        split_lo(n0 + c, g, 6)
                for f in range(GF):
                    for h in range(NH):
                        q = f * NH + h
                        if ada:
                            ada_tile(g + 2, 2 * q)
                            ada_tile(g + 2, 2 * q + 1)
                        if h == 1:
                            split_lo(n0 + 3 + 2 * f, g, 6)
                        dve.wait_ge(job_done, J + 2 * q + 2)
                        dve.wait_ge(aevac, A + q + 1)
                        nc.vector.tensor_tensor(TmpG[:, h, :], TmpA[:, h, :], PS[:, (2 * q + 1) % BANKS, :], ALU.mult)\
                            .then_inc(evac, 1)
                        g_lo(f, h, G + q + 1)
                    if not (final and f == GF - 1):
                        split_lo(n0 + 4 + 2 * f, g, 6)
                if ada:
                    ada_bias(g + 2)
                if first and n == 0:
                    gate(0, GT1, 0.5)
                    dve.wait_ge(scales, 2)
                job_bank = 8
                add_outs(J + 8, n, q0)

            job_bank = 0
            nc.vector.memset(Ones[:], 1.0)
            nc.vector.memset(Mean[:], 1.0 / D)
            nc.vector.memset(MeanG[:], 0.0).then_inc(mset, 1)
            nc.vector.memset(EpsC[:, 1:2], SUB_EPS)
            dve.wait_ge(mset, 1)
            for gi in range(2):
                nc.vector.memset(MeanG[gi * DH:(gi + 1) * DH, gi:gi + 1], 1.0 / DH)
            nc.vector.memset(EpsC[:, 0:1], EPS).then_inc(consts, 1)
            dve.wait_ge(lam_loaded, 16)
            nc.vector.tensor_tensor(LamP[:], Lam4[:, 0:2, :], Lam4[:, 2:4, :], ALU.mult).then_inc(lam_done, 1)
            dve.wait_ge(lam_done, 1)
            nc.vector.tensor_reduce(LamS[:, 0:2], LamP[:], AX.X, ALU.add).then_inc(lam_done, 1)
            for k in range(1, KT):
                for h in range(NH):
                    dve.wait_ge(sq_done, NH * k + h + 1)
                    if k > 1:
                        dve.wait_ge(ssum, NH * (k - 2) + h + 1)
                    nc.vector.tensor_tensor(SqSum[:, h, :], SqSum[:, h, :], Sq[:, h, :], ALU.add).then_inc(ssum, 1)
            dve.wait_ge(lam_exp, 1)
            nc.vector.tensor_tensor(LamS[:, 4:5], LamS[:, 3:4], LamS[:, 2:3], ALU.subtract).then_inc(lam_done, 1)
            dve.wait_ge(lam_done, 3)
            nc.vector.tensor_scalar(LamS[:, 5:6], LamS[:, 4:5], -LAMBDA_INIT, None, ALU.add).then_inc(lam_done, 1)
            nc.vector.tensor_scalar(SubG[:], col("subln"), 1.0 - LAMBDA_INIT, None, ALU.mult).then_inc(lam_done, 1)
            def xn(q, k):
                nc.vector.tensor_tensor(XN[:, k, half(q)], X[:, k, half(q)], PS[:, 7 - q, :], ALU.mult).then_inc(xn_done, 1)

            ada_tile(SC1, 0)
            for q in range(NH):
                spread(q)
            for k in range(1, KT):
                ada_tile(SC1, k)
                if k == 2:
                    dve.wait_ge(bcast_done, NH)
                if k >= 2:
                    xn(0, k - 2)
            for k in (KT - 2, KT - 1):
                xn(0, k)
            for n in range(RING - 1):
                split_lo(n)
            ada_bias(SH1, 4)
            ada_bias(SC1, 5)
            scale(0, SC1, "g1")
            dve.wait_ge(scales, 1)
            for q in range(NH):
                for k in range(KT):
                    at = q * KT + k
                    if at >= 2:
                        dve.wait_ge(h_ready, at - 1)
                    nc.vector.tensor_scalar(TmpG[:, k % 2, :], XN[:, k, half(q)], Scale[:, 0, k:k + 1],
                                            Mod[:, SH1 * KT + k:SH1 * KT + k + 1], ALU.mult, ALU.add).then_inc(hf_done, 1)
                    dve.wait_ge(hf_done, at + 1)
                    norm_lo(q, k)
                    if q == 0:
                        xn(1, k)
                if q == 0:
                    split_lo(RING - 1)

            ffn_group("ffn1", 0, 0, 0, first=True, ada=True)
            with dve.Fori(1, SECTIONS - 2) as g:
                ffn_group("ffn1", g, 0, 0, ada=True)
            for n, section, gain in ((1, SC2, "g2"), (2, SC3, "g3"), (3, SCF, "gf")):
                scale(n, section, gain)
            gate(1, GT2, 1.0)
            gate(2, GT3, 0.5)
            dve.wait_ge(scales, 7)
            ffn_group("ffn1", NG - 2, 0, 0)
            ffn_group("ffn1", NG - 1, 0, 0, q0=2)
            norm_tiles(2, (U_CONV + 1, U_CONV + 2))

            nc.vector.memset(CU[:, 0:2], 0.0).then_inc(halo, 1)
            dve.wait_ge(halo, 1)
            for cg in range(2):
                J, E, A, G = JOBS["conv"] + 28 * cg, EVAC["conv"] + 24 * cg, AEVAC["conv"] + 4 * cg, GDONE["conv"] + 4 * cg
                n0 = U_CONV + 8 * cg
                if cg:
                    for c in (1, 2):
                        split_lo(n0 + c)
                for q in range(4):
                    jt, h, cq = q // 2, q % 2, 4 * cg + q
                    tile = 2 * cg + jt
                    dve.wait_ge(job_done, J + 3 * q + 2)
                    dve.wait_ge(aevac, A + q + 1)
                    nc.vector.tensor_tensor(CU[:, 2 + h * HALF:2 + (h + 1) * HALF], TmpA[:, h, :],
                                            PS[:, (3 * q + 1) % BANKS, :], ALU.mult).then_inc(evac, 1)
                    if h == 1:
                        split_lo(n0 + 3 * jt + 4)
                    dve.wait_ge(evac, E + 2 * q + 1)
                    nc.vector.tensor_scalar(CT[:, half(h)], CU[:, 2 + h * HALF:2 + (h + 1) * HALF],
                                            col("conv_w", 2 * 4 + tile), None, ALU.mult).then_inc(ct_done, 1)
                    for tap in (1, 0):
                        dve.wait_ge(ct_done, cq * 3 + 2 - tap)
                        nc.vector.scalar_tensor_tensor(CT[:, half(h)], CU[:, tap + h * HALF:tap + (h + 1) * HALF],
                                                       col("conv_w", tap * 4 + tile), CT[:, half(h)],
                                                       ALU.mult, ALU.add).then_inc(ct_done, 1)
                    dve.wait_ge(job_done, J + 3 * q + 3)
                    dve.wait_ge(ct_done, cq * 3 + 3)
                    nc.vector.tensor_tensor(CT[:, half(h)], CT[:, half(h)], PS[:, (3 * q + 2) % BANKS, :], ALU.mult)\
                        .then_inc(evac, 1)
                    if h == 1:
                        split_lo(n0 + 3 * jt + 5)
                    dve.wait_ge(croot_done, cq + 1)
                    nc.vector.reciprocal(Inv[:, 0:8], Root[:, 0:8]).then_inc(cinv_done, 1)
                    dve.wait_ge(cinv_done, cq + 1)
                    nc.vector.tensor_copy(Spread[:, h, :].rearrange("p (b c) -> p b c", b=8),
                                          Inv[:, 0:8].unsqueeze(2).to_broadcast([P, 8, DH])).then_inc(cspread_done, 1)
                    if h == 0:
                        split_lo(n0 + 3 * jt + 3)
                    dve.wait_ge(cbc_done, cq + 1)
                    nc.vector.scalar_tensor_tensor(TmpG[:, h, :], CT[:, half(h)], col("conv_g", tile), PS[:, 7, :],
                                                   ALU.mult, ALU.mult).then_inc(cg_done, 1)
                    g_lo(jt, h, G + q + 1)
                job_bank = 12
                add_outs(J + 12, 1)

            for c in range(1, 8):
                split_lo(U_Q0 + c)
            for t in range(1, QB, 2):
                dve.wait_ge(job_done, JOBS["v"] + 4 + t + 1)
                nc.vector.tensor_copy(V[:, t, :], PS[:, t, :]).then_inc(evac, 1)

            def maxima(i, at):
                for c in range(2):
                    dve.wait_ge(score_done, at * 2 + c + 1)
                    nc.vector.tensor_tensor(scores(c, i, i + 1), scores(c, i, i + 1), mask, ALU.add).then_inc(masked, 1)
                    dve.wait_ge(masked, at * 2 + c + 1)
                    nc.vector.tensor_reduce(NMax[:, c:c + 1], scores(c, 0, i + 1), AX.X, ALU.max, negate=True)\
                        .then_inc(max_done, 1)

            def difference(i, at, rounds):
                w = P * (i + 1)
                dve.wait_ge(exp_done, at * 2 + 2)
                nc.vector.reciprocal(RSum[:, i, :], Sum[:]).then_inc(rsum_done, 1)
                dve.wait_ge(rsum_done, at + 1)
                nc.vector.scalar_tensor_tensor(Ratio[:], RSum[:, i, 1:2], LamS[:, 5:6], Sum[:, 0:1], ALU.mult, ALU.mult)\
                    .then_inc(ratio_done, 1)
                dve.wait_ge(ratio_done, at + 1)
                if rounds is not None:
                    dve.wait_ge(tr_done, rounds)
                nc.vector.scalar_tensor_tensor(PR[:, 2, 0:w], PR[:, 1, 0:w], Ratio[:, 0:1], PR[:, 0, 0:w],
                                               ALU.mult, ALU.add).then_inc(diff_done, 1)

            def norm_o(count):
                dve.wait_ge(oroot_done, count)
                nc.vector.reciprocal(Inv[:, 0:QB], Root[:, 0:QB]).then_inc(oinv_done, 1)
                dve.wait_ge(oinv_done, count)
                nc.vector.tensor_tensor(O[:], O[:], Inv[:, 0:QB].unsqueeze(2).to_broadcast([P, QB, P]), ALU.mult)\
                    .then_inc(onorm_done, 1)

            def o_lo(h, bank, count):
                dve.wait_ge(ghi, count + h + 1)
                nc.vector.scalar_tensor_tensor(Gl[:, 0, half(h)], PS[:, bank, :], SubG[:, 0:1],
                                               Gh[:, 0, half(h)].bitcast(F32), ALU.mult, ALU.subtract).then_inc(g_ready, 1)

            def body(hh, nq, ny, prev, nxt):
                nonlocal job_bank
                J = JOBS["att"] + (hh * 20 - 16 if prev else 0)
                i3, per = (hh, 3) if prev and nxt else (0, 0)
                steps = STEP_OF_JOB if prev else STEP_OF_JOB_FIRST
                tile = 0
                for i in range(QB):
                    at = hh * QB + i
                    difference(i, at, hh * ALL_ROUNDS + (DT_COUNT[i - 1] if i else 0) if i or prev else None)
                    if i < QB - 1 or nxt:
                        maxima((i + 1) % QB, at + 1)
                    if prev and i == 0:
                        norm_o(hh)
                    if prev and i == 1:
                        for h in range(NH):
                            o_lo(h, (4 if nxt else 6) + h, GDONE["att"] + hh * NH - NH)
                    if nxt and i - 1 in steps and steps.index(i - 1) % 2:
                        split_lo(nq + 3 + steps.index(i - 1) // 2, i3, per)
                    if nxt and i == QB - 2:
                        dve.wait_ge(rope_done, hh * 4 + 8)
                        dve.wait_ge(score_done, hh * (2 * QB) + 2 * QB)
                        nc.vector.tensor_copy(QK[:, 1, 0:S], NextK[:]).then_inc(k_moved, 1)
                    for _ in range((TILES if nxt else TILES_LAST)[i] if prev else 0):
                        add_out(J + (4 if nxt else 0), 1, tile, 6 + tile % 2)
                        tile += 1
                if prev and nxt:
                    split_lo(ny + 3, i3, per)

            maxima(0, 0)
            split_lo(U_HEAD)
            body(0, U_Q1, None, False, True)
            with dve.Fori(1, HEADS - 1) as hh:
                body(hh, U_HEAD - 3, U_HEAD - 1, True, True)
            body(HEADS - 1, None, U_WO2, True, False)
            left = TILES_LAST[-1]
            for t in range(NH * KT - left, NH * KT):
                if t == NH * KT - 2:
                    norm_o(HEADS)
                add_out(JOBS["ffn2"] - 2 * 16, 1, t, 6 + t % 2)
            for h in range(NH):
                o_lo(h, 4 + h, GDONE["att"] + (HEADS - 1) * NH)
            split_lo(U_WO2 + 3)
            job_bank = 0
            add_outs(JOBS["ffn2"] - 16, 1, 4)
            norm_tiles(4, (U_FFN2 + 2,))

            ffn_group("ffn2", 0, U_FFN2, 2, first=True)
            with dve.Fori(1, NG - 1) as g:
                ffn_group("ffn2", g, U_FFN2, 2)
            ffn_group("ffn2", NG - 1, U_FFN2, 2, final=True, q0=6)
            norm_tiles(6, final=True)

        @block.tensor
        def _(pe):
            def mm(out, lhs, rhs, first, last):
                return nc.tensor.matmul(out, lhs, rhs, start=first, stop=last)

            def products(bank, n, h, ks):
                for k in ks:
                    s, w = n % RING, blk(k)
                    mm(PS[:, bank, :], Wh[:, s, w], Hh[:, k, half(h)], k == 0, False)
                    mm(PS[:, bank, :], Wh[:, s, w], Hl[:, k, half(h)], False, False)
                    made = mm(PS[:, bank, :], Wl[:, s, w], Hh[:, k, half(h)], False, k == KT - 1)
                    if k == KT - 1:
                        made.then_inc(job_done, 1)

            def project(bank, n, h):
                products(bank, n, h, range(KT))

            LAG = 3

            def project_new(bank, n, h, q):
                for k in range(KT + LAG):
                    if k < KT:
                        pe.wait_ge(h_ready, q * KT + k + 1)
                        products(bank, n, h, (k,))
                    if k >= LAG:
                        if k == LAG:
                            pe.wait_ge(lo_done, n + 2)
                        products(bank + 1, n + 1, h, (k - LAG,))
                    if k == 2 and q % 2 == 0 and EARLY.get(q):
                        mean(q + 1)
                    if k == (KT if EARLY.get(q) else 4) and q % 2 == 0 and q:
                        bcast(q + 1)

            def out_job(bank, ns, t):
                h, d = t // KT, t % KT
                for f, n in enumerate(ns):
                    s, w = n % RING, blk(d)
                    mm(PS[:, bank, :], Wh[:, s, w], Gh[:, f, half(h)], f == 0, False)
                    mm(PS[:, bank, :], Wh[:, s, w], Gl[:, f, half(h)], False, False)
                    made = mm(PS[:, bank, :], Wl[:, s, w], Gh[:, f, half(h)], False, f == len(ns) - 1)
                made.then_inc(job_done, 1)

            def mean(q):
                pe.wait_ge(ssum, (q + 1) * (KT - 1) if q >= NH else NH * (KT - 1))
                for b in range(4):
                    made = mm(PS[:, 6, b:b + 1], SqSum[:, q % NH, blk(b)], Mean[:], True, True)
                made.then_inc(mean_done, 1)

            def bcast(q):
                pe.wait_ge(spread_done, q + 1)
                for b in range(4):
                    made = mm(PS[:, 7 - q % 2, blk(b)], Spread[:, q % NH, blk(b)], ident, True, True)
                made.then_inc(bcast_done, 1)

            def ada_cols(s, bank=7):
                pe.wait_ge(ada_used, s * KT)
                for c in range(KT):
                    made = mm(PS[:, bank, c:c + 1], AdaSum[:, blk(c)], Ones[:], True, True)
                made.then_inc(cols_done, 1)

            def norm_between(q0, t, at, then):
                if q0 is not None and t == at:
                    mean(q0)
                if q0 is not None and t == then:
                    bcast(q0)

            def ffn_group(phase, g, n0, first=False, ada=False, q=None, q0=None):
                J, E, A, G = JOBS[phase] + g * 24, EVAC[phase] + g * 20, AEVAC[phase] + g * 4, GDONE[phase] + g * 4

                def bank_free(L):
                    if L < BANKS:
                        if not first:
                            pe.wait_ge(evac, E - 5 + L)
                        elif EVAC[phase]:
                            pe.wait_ge(evac, E)
                    elif L < BANKS + 8:
                        pe.wait_ge(*((evac, E + (L - BANKS) // 2 + 1) if L % 2 else (aevac, A + (L - BANKS) // 2 + 1)))
                    else:
                        pe.wait_ge(evac, E + 4 + L - 14 + 1)

                for f in range(GF):
                    for h in range(NH):
                        for w in range(2):
                            L = 4 * f + 2 * h + w
                            bank_free(L)
                            if q is not None and f == 0:
                                if w == 0:
                                    pe.wait_ge(lo_done, n0 + 1)
                                    bank_free(L + 1)
                                    project_new(L, n0, h, q + h)
                                continue
                            if h == 0:
                                pe.wait_ge(lo_done, n0 + 2 * f + w + 1 + g * 6)
                            project(L % BANKS, n0 + 2 * f + w, h)
                if ada:
                    ada_cols(g + 2)
                pe.wait_ge(lo_done, n0 + 6 + g * 6)
                for t in range(NH * KT):
                    bank_free(8 + t)
                    if t % KT == 0:
                        pe.wait_ge(g_ready, G + 3 + t // KT)
                    out_job((8 + t) % BANKS, (n0 + 4, n0 + 5), t)
                    norm_between(q0, t, KT + 1, KT + 4)

            pe.wait_ge(c_act, 1)
            for k in range(KT):
                pe.wait_ge(first_loaded[k], 16)
                for c in range(D // HALF):
                    made = mm(PS[0:1, c, :], CAct[:, k:k + 1], AdaFirst[:, k, half(c)], k == 0, k == KT - 1)
                made.then_inc(row_used, 1)
                if k == 4:
                    pe.wait_ge(consts, 1)
                    mean(0)
                if k == 6:
                    pe.wait_ge(root_done, 1)
                    mean(1)
            pe.wait_ge(square_loaded, 16)
            bcast(0)
            pe.wait_ge(root_done, 2)
            bcast(1)
            pe.wait_ge(row_done, 1)
            for c in range(KT):
                made = mm(PS[:, 4, c:c + 1], AdaRow[0:1, blk(c)], Ones[0:1, :], True, True)
            made.then_inc(cols_done, 1)
            ada_cols(SC1, 5)
            ffn_group("ffn1", 0, 0, first=True, ada=True, q=0)
            with pe.Fori(1, SECTIONS - 2) as g:
                ffn_group("ffn1", g, 0, ada=True)
            ffn_group("ffn1", NG - 2, 0)
            ffn_group("ffn1", NG - 1, 0, q0=2)

            for cg in range(2):
                J, E, A, G = JOBS["conv"] + 28 * cg, EVAC["conv"] + 24 * cg, AEVAC["conv"] + 4 * cg, GDONE["conv"] + 4 * cg
                n0 = U_CONV + 8 * cg

                def reader(L):
                    q, w = L // 3, L % 3
                    if L >= 12:
                        return evac, E + 8 + L - 12 + 1
                    return (evac, E + 2 * q + w) if w else (aevac, A + q + 1)

                def group_mean(q):
                    pe.wait_ge(csq_done, 4 * cg + q + 1)
                    for b in range(4):
                        made = mm(PS[:, 6, 2 * b:2 * b + 2], Sq[:, q % 2, blk(b)], MeanG[:], True, True)
                    made.then_inc(cmean_done, 1)

                def group_bcast(q):
                    pe.wait_ge(cspread_done, 4 * cg + q + 1)
                    for b in range(4):
                        made = mm(PS[:, 7, blk(b)], Spread[:, q % 2, blk(b)], ident, True, True)
                    made.then_inc(cbc_done, 1)

                for L in range(12):
                    q, w = L // 3, L % 3
                    if L < BANKS:
                        pe.wait_ge(evac, E)
                    else:
                        pe.wait_ge(*reader(L - BANKS))
                    if cg == 0 and q < 2 and w < 2:
                        if w == 0:
                            pe.wait_ge(lo_done, n0 + 1)
                            project_new(L, n0, q, 2 + q)
                    else:
                        if q % 2 == 0:
                            pe.wait_ge(lo_done, n0 + 3 * (q // 2) + w + 1)
                        project(L % BANKS, n0 + 3 * (q // 2) + w, q % 2)
                    if q and w == 0:
                        group_mean(q - 1)
                    if q and w == 1:
                        group_bcast(q - 1)
                pe.wait_ge(lo_done, n0 + 8)
                for t in range(NH * KT):
                    pe.wait_ge(*reader(12 + t - BANKS))
                    if t % KT == 0:
                        pe.wait_ge(g_ready, G + 3 + t // KT)
                    out_job((12 + t) % BANKS, (n0 + 6, n0 + 7), t)
                    if t == 0:
                        group_mean(3)
                    if t == 3:
                        group_bcast(3)

            for j in range(4):
                if j < 2:
                    pe.wait_ge(evac, EVAC["v"] - (4 if j == 0 else 0))
                if j % 2 == 0:
                    pe.wait_ge(lo_done, U_Q0 + j // 2 + 1)
                project(4 + j, U_Q0 + j // 2, j % 2)

            for u in range(4):
                pe.wait_ge(lo_done, U_V + u + 1)
                s = (U_V + u) % RING
                for kk in range(2):
                    k, w = 2 * u + kk, half(kk)
                    for t in range(QB):
                        if k == 0 and t >= 4:
                            pe.wait_ge(rraw, t - 3)
                        mm(PS[:, t, :], Hh[:, k, blk(t)], Wh[:, s, w], k == 0, False)
                        mm(PS[:, t, :], Hl[:, k, blk(t)], Wh[:, s, w], False, False)
                        made = mm(PS[:, t, :], Hh[:, k, blk(t)], Wl[:, s, w], False, k == KT - 1)
                        if k == KT - 1:
                            made.then_inc(job_done, 1)
                if u < 3:
                    made.then_inc(v_used, 1)

            def score(i, at):
                for c in range(2):
                    if not (isinstance(at, int) and at == 0):
                        pe.wait_ge(exp_done, at * 2 - 1 + c)
                    part = slice(c * DH, (c + 1) * DH)
                    for a in range(0, P * (i + 1), HALF):
                        b = min(a + HALF, P * (i + 1))
                        made = mm(PS[:, 2 * c + a // HALF, 0:b - a], QK[part, 0, blk(i)], QK[part, 1, a:b], True, True)
                    made.then_inc(score_done, 1)

            def values(i, hh):
                pe.wait_ge(dt_done, hh * ALL_ROUNDS + DT_COUNT[i])
                if i:
                    pe.wait_ge(o_done, hh * QB + i)
                for b in range(i + 1):
                    made = mm(PS[:, 5, 0:P], DT[:, blk(b)], V[:, b, bass.ts(hh, P)], b == 0, b == i)
                made.then_inc(pv_done, 1)

            def turn_o(banks, count):
                pe.wait_ge(onorm_done, count)
                for i in range(QB):
                    made = nc.tensor.transpose(PS[:, banks + i // 4, blk(i % 4)], O[:, i, :], ident)
                    if i % 4 == 3:
                        made.then_inc(ot_done, 1)

            def body(hh, nq, ny, prev, nxt):
                E, G = EVAC["att"] + hh * 16 - 16, GDONE["att"] + hh * NH - NH
                per = 3 if prev and nxt else 0
                chunk, tile = 0, 0

                def chunks(n):
                    nonlocal chunk
                    for _ in range(n):
                        j, k = chunk // KT, chunk % KT
                        if k == 0:
                            if j == 0:
                                pe.wait_ge(rraw, hh * 4 + 4)
                                if prev:
                                    pe.wait_ge(evac, E)
                            elif j >= 2:
                                pe.wait_ge(rraw, hh * 4 + 4 + j - 1)
                            if j % 2 == 0:
                                pe.wait_ge(lo_done, nq + j // 2 + 1 + (hh * per if per else 0))
                        products(6 + j % 2, nq + j // 2, j % 2, (k,))
                        chunk += 1

                def tiles(n):
                    nonlocal tile
                    for _ in range(n):
                        t = tile
                        if t == 0:
                            pe.wait_ge(lo_done, ny + 1 + (hh * per if per else 0))
                            if nxt:
                                pe.wait_ge(rraw, hh * 4 + 8)
                        if t % KT == 0:
                            pe.wait_ge(g_ready, G + (t // KT + 1 if nxt else NH))
                        if t >= 2:
                            pe.wait_ge(evac, E + t - 1)
                        out_job(6 + t % 2, (ny,), t)
                        tile += 1

                for i in range(QB):
                    at = hh * QB + i
                    if i == 0 and not nxt:
                        values(QB - 1, hh - 1)
                    if i < QB - 1 or nxt:
                        if i == QB - 1:
                            pe.wait_ge(q_moved, hh + 1)
                            pe.wait_ge(k_moved, hh + 1)
                        score((i + 1) % QB, at + 1)
                    n = (CHUNKS if prev else CHUNKS_FIRST)[i] if nxt else 0
                    if prev and i == 1:
                        early = min(1, n)
                        chunks(early)
                        if nxt:
                            pe.wait_ge(dt_done, hh * ALL_ROUNDS + 1)
                        turn_o(4 if nxt else 6, hh)
                        n -= early
                    if prev and nxt and i == 0:
                        chunks(FIRST)
                        values(QB - 1, hh - 1)
                        n -= FIRST
                    chunks(n)
                    n = (TILES if nxt else TILES_LAST)[i] if prev else 0
                    split = [min(2, n), int(n > 2), int(n > 3), max(n - 4, 0)]
                    tiles(split[0])
                    if i:
                        if i == 1 and prev and nxt:
                            pe.wait_ge(g_ready, G + NH)
                        values(i - 1, hh)
                    tiles(split[1])
                    pe.wait_ge(diff_done, at + 1)
                    for r in range(ROUNDS[i]):
                        before = DT_COUNT[i] - ROUNDS[i] + r
                        if before or prev:
                            pe.wait_ge(dt_done, hh * ALL_ROUNDS + before)
                        for b in range(4 * r, min(4 * r + 4, i + 1)):
                            made = nc.tensor.transpose(PS[:, 4, blk(b % 4)], PR[:, 2, blk(b)], ident)
                        made.then_inc(tr_done, 1)
                        if r == 0:
                            tiles(split[2])
                    tiles(split[3])

            pe.wait_ge(rope_done, 4)
            pe.wait_ge(aevac, AEVAC["att"])
            pe.wait_ge(evac, EVAC["att"])
            score(0, 0)
            body(0, U_Q1, None, False, True)
            with pe.Fori(1, HEADS - 1) as hh:
                body(hh, U_HEAD - 3, U_HEAD - 1, True, True)
            body(HEADS - 1, None, U_WO2, True, False)
            values(QB - 1, HEADS - 1)
            for t in range(NH * KT - TILES_LAST[-1], NH * KT):
                pe.wait_ge(evac, EVAC["ffn2"] - 2 * 16 + t - 1)
                out_job(6 + t % 2, (U_WO2,), t)
            turn_o(4, HEADS)
            pe.wait_ge(lo_done, U_WO2 + 2)
            for t in range(NH * KT):
                if t % KT == 0:
                    pe.wait_ge(g_ready, GDONE["ffn2"] - NH + t // KT + 1)
                if t == 4:
                    pe.wait_ge(g_ready, GDONE["ffn2"])
                if t >= BANKS:
                    pe.wait_ge(evac, EVAC["ffn2"] - 16 + t - BANKS + 1)
                out_job(t % BANKS, (U_WO2 + 1,), t)
                norm_between(4, t, KT + 3, KT + 7)
            mean(5)

            ffn_group("ffn2", 0, U_FFN2, first=True, q=4)
            with pe.Fori(1, NG - 1) as g:
                ffn_group("ffn2", g, U_FFN2)
            ffn_group("ffn2", NG - 1, U_FFN2, q0=6)
            mean(7)
            bcast(7)


def kernel(**inputs):
    import numpy as np
    import concourse.bacc as bacc
    from concourse.bass_utils import run_bass_kernel_spmd

    a = {k: np.asarray(v) for k, v in inputs.items()}

    def cols(w, at):
        return w[:, at:at + P].reshape(KT, P, P).transpose(1, 0, 2).reshape(P, D)

    def rows(w, n):
        return w[n * P:(n + 1) * P]

    w_in, w_out = a["w_in"][0], a["w_out"][0]
    width = HEADS * P
    V0, B0, C0, U0 = 2 * width, 3 * width, 4 * width, 5 * width
    units = []

    def ffn_units(w1, w3, w2):
        for g in range(NG):
            for f in range(GF * g, GF * g + GF):
                units.extend([cols(w1, f * P), cols(w3, f * P)])
            units.extend(rows(w2, f) for f in range(GF * g, GF * g + GF))

    ffn_units(a["ffn1_w1"][0], a["ffn1_w3"][0], a["ffn1_w2"][0])
    for cg in range(2):
        for t in (2 * cg, 2 * cg + 1):
            units.extend(cols(w_in, at + t * P) for at in (U0, C0, B0))
        units.extend(rows(w_out, HEADS + t) for t in (2 * cg, 2 * cg + 1))
    def qk_units(h):
        return [cols(w_in, h * P), cols(w_in, width + h * P)]

    units.extend(qk_units(0))
    for u in range(4):
        units.append(w_in[2 * u * P:(2 * u + 2) * P, V0:V0 + width].reshape(2, P, width).transpose(1, 0, 2).reshape(P, D))
    units.extend(qk_units(1))
    for h in range(2):
        units.extend(qk_units(h + 2) + [rows(w_out, h)])
    units.extend([rows(w_out, 2), rows(w_out, 3)])
    ffn_units(a["ffn2_w1"][0], a["ffn2_w3"][0], a["ffn2_w2"][0])

    ada_w = np.concatenate([a["w_ada"][0], a["w_ada_final"]], axis=1)
    ada_b = np.concatenate([a["b_ada"][0], a["b_ada_final"]])

    def down(v):
        return v.reshape(-1, P).T

    inv = (1.0 / (np.float32(10000.0) ** (np.arange(0, DH, 2, dtype=np.float32) / np.float32(DH)))).astype(np.float32)
    ang = (np.arange(S, dtype=np.float32)[:, None] * inv[None, :]).astype(np.float32)
    cos, sin = np.cos(ang).T, np.sin(ang).T
    rope = np.stack([np.concatenate([cos] * 4), np.concatenate([-sin, sin] * 2)], axis=1)
    below = np.where(np.arange(P)[None, :] <= np.arange(P)[:, None], 0.0, MASKED)
    arrays = {
        "units": np.stack(units),
        "ada": ada_w.reshape(KT, P, SECTIONS, D).transpose(2, 0, 1, 3).reshape(SECTIONS * KT, P, D),
        "x_t": a["x"][0].T.reshape(KT, P, S),
        "cols": np.concatenate([down(ada_b), down(a["c"][0]), down(a["g_ffn1"][0]), down(a["g_mix"][0]),
                                down(a["g_ffn2"][0]), down(a["g_final"]), down(a["subln_g"][0]),
                                down(a["conv_w"][0].reshape(-1)), down(a["conv_norm_g"][0])], axis=1),
        "lam": np.broadcast_to(np.stack([a["lambda_q1"][0], a["lambda_q2"][0], a["lambda_k1"][0],
                                         a["lambda_k2"][0]])[None], (P, 4, DH)),
        "rope": rope.astype(np.float32),
        "square": np.stack([np.eye(P), below], axis=1).astype(np.float32),
    }
    arrays = {k: np.ascontiguousarray(v) for k, v in arrays.items()}
    nc = bacc.Bacc("TRN2", target_bir_lowering=False, num_devices=1)
    aps = [nc.dram_tensor(k, v.shape, mybir.dt.from_np(v.dtype), kind="ExternalInput").ap() for k, v in arrays.items()]
    out_t = nc.dram_tensor("out_t", (KT, P, S), F32, kind="ExternalOutput").ap()
    program(nc, *aps, out_t)
    got = run_bass_kernel_spmd(nc, [arrays], core_ids=[0])
    return np.ascontiguousarray(got.results[0]["out_t"].reshape(D, S).T)[None]
```
